# Optimizing a Trainium2 kernel written in Bass

```python
import jax, jax.numpy as jnp
from jax import lax
import numpy as np

D_MODEL = 2048
BATCH = 1
SEQ = 512
DEPTH = 1
DEC_BATCH = 8
DEC_SEQ = 4
PAST_LEN = 4096
PAGE_SIZE = 128

D_RNN = D_MODEL // 2
RNN_HEADS = 8
RNN_HEAD_DIM = D_RNN // RNN_HEADS
RNN_CONV_W = 4
LRU_C = 8.0
D_CONV = D_MODEL // 2
CONV_W = 31
N_KEYS = 128
N_EXPERTS = N_KEYS * N_KEYS
PEER_HEADS = 8
PEER_TOPK = 16
D_KEY = 256
D_HALF = D_KEY // 2
PEER_BLOCK = 128
EPS = 1e-6
IN_COLS = 2 * D_RNN + 2 * D_CONV + 2 * D_MODEL

kernel_name = 'hawk_conformer_peer_hybrid_step'

def _rmsnorm(x, g):
    xf = x.astype(jnp.float32)
    r = xf * lax.rsqrt(jnp.mean(xf * xf, axis=-1, keepdims=True) + EPS)
    return (r * g.astype(jnp.float32)).astype(x.dtype)

def _layernorm(x, g, b):
    xf = x.astype(jnp.float32)
    mu = jnp.mean(xf, axis=-1, keepdims=True)
    xc = xf - mu
    var = jnp.mean(xc * xc, axis=-1, keepdims=True)
    return (xc * lax.rsqrt(var + EPS) * g.astype(jnp.float32) + b.astype(jnp.float32)).astype(x.dtype)

def _split_cols(z):
    idx = [D_RNN, 2 * D_RNN, 2 * D_RNN + D_CONV, 2 * D_RNN + 2 * D_CONV,
           2 * D_RNN + 2 * D_CONV + D_MODEL]
    return jnp.split(z, idx, axis=-1)

def _causal_dwconv(x, buf, w, b):
    width, c = w.shape
    xp = jnp.concatenate([buf.astype(x.dtype), x], axis=1)
    y = lax.conv_general_dilated(xp, w.astype(x.dtype)[:, None, :], window_strides=(1,),
                                 padding='VALID', dimension_numbers=('NWC', 'WIO', 'NWC'),
                                 feature_group_count=c)
    return y + b.astype(x.dtype), xp[:, xp.shape[1] - (width - 1):]

def _rglru(xc, h0, w_r, b_r, w_i, b_i, lam):
    bsz, t, _ = xc.shape
    f32 = jnp.float32
    xf = xc.astype(f32)
    xh = xf.reshape(bsz, t, RNN_HEADS, RNN_HEAD_DIM)
    r = jax.nn.sigmoid(jnp.einsum('bthi,hij->bthj', xh, w_r.astype(f32)).reshape(bsz, t, D_RNN) + b_r.astype(f32))
    ig = jax.nn.sigmoid(jnp.einsum('bthi,hij->bthj', xh, w_i.astype(f32)).reshape(bsz, t, D_RNN) + b_i.astype(f32))
    log_a = -LRU_C * jax.nn.softplus(-lam.astype(f32)) * r
    a = jnp.exp(log_a)
    bterm = jnp.sqrt(-jnp.expm1(2.0 * log_a)) * (ig * xf)

    def combine(lhs, rhs):
        a1, b1 = lhs
        a2, b2 = rhs
        return a1 * a2, a2 * b1 + b2

    a_cum, b_cum = lax.associative_scan(combine, (a, bterm), axis=1)
    h = a_cum * h0.astype(f32)[:, None, :] + b_cum
    return h, h[:, -1]

def _peer(xn, w_q, keys1, keys2, u_tab, v_tab):
    bsz, t, d = xn.shape
    n = bsz * t
    nb = -(-n // PEER_BLOCK)
    flat = jnp.pad(xn.reshape(n, d), ((0, nb * PEER_BLOCK - n), (0, 0))).reshape(nb, PEER_BLOCK, d)
    f32 = jnp.float32

    def block(xb):
        q = (xb @ w_q).astype(f32).reshape(PEER_BLOCK, PEER_HEADS, 2, D_HALF)
        s1 = jnp.einsum('thd,hkd->thk', q[:, :, 0], keys1.astype(f32))
        s2 = jnp.einsum('thd,hkd->thk', q[:, :, 1], keys2.astype(f32))
        v1, i1 = lax.top_k(s1, PEER_TOPK)
        v2, i2 = lax.top_k(s2, PEER_TOPK)
        cand = (v1[..., :, None] + v2[..., None, :]).reshape(PEER_BLOCK, PEER_HEADS, PEER_TOPK * PEER_TOPK)
        sv, si = lax.top_k(cand, PEER_TOPK)
        e = (jnp.take_along_axis(i1, si // PEER_TOPK, axis=-1) * N_KEYS
             + jnp.take_along_axis(i2, si % PEER_TOPK, axis=-1))
        g = jax.nn.softmax(sv, axis=-1)
        u = u_tab[e]
        act = jax.nn.gelu(jnp.einsum('thkd,td->thk', u, xb).astype(f32))
        v = v_tab[e]
        return jnp.einsum('thk,thkd->td', (g * act).astype(xb.dtype), v)

    out = lax.map(block, flat).reshape(nb * PEER_BLOCK, d)[:n]
    return out.reshape(bsz, t, d)

def _trunk(x, rnn_conv, rnn_h, cm_conv, p):
    new_rc, new_h, new_cc = [], [], []
    for l in range(DEPTH):
        xn = _rmsnorm(x, p['g_mix'][l])
        xr, yr, ca, cb, ga, gb = _split_cols(xn @ p['w_in'][l])
        xc, rc = _causal_dwconv(xr, rnn_conv[l], p['w_rconv'][l], p['b_rconv'][l])
        h, h_last = _rglru(xc, rnn_h[l], p['w_r'][l], p['b_r'][l], p['w_i'][l], p['b_i'][l], p['lam'][l])
        branch_a = (h.astype(x.dtype) * jax.nn.gelu(yr)) @ p['w_a'][l]
        glu = ca * jax.nn.sigmoid(cb)
        dc, cc = _causal_dwconv(glu, cm_conv[l], p['w_cconv'][l], p['b_cconv'][l])
        branch_b = jax.nn.silu(_layernorm(dc, p['ln_g'][l], p['ln_b'][l])) @ p['w_b'][l]
        merged = jax.nn.sigmoid(ga) * branch_a + jax.nn.sigmoid(gb) * branch_b
        x = x + merged @ p['w_out'][l]
        x = x + _peer(_rmsnorm(x, p['g_ffn'][l]), p['w_q'][l], p['keys1'][l], p['keys2'][l],
                      p['u_tab'][l], p['v_tab'][l])
        new_rc.append(rc.astype(rnn_conv.dtype))
        new_h.append(h_last.astype(rnn_h.dtype))
        new_cc.append(cc.astype(cm_conv.dtype))
    y = _rmsnorm(x, p['g_final'])
    return y, jnp.stack(new_rc), jnp.stack(new_h), jnp.stack(new_cc)

def setup_inputs(seed: int = 0) -> dict:
    key = jax.random.key(seed)
    ks = jax.random.split(key, 32)
    nrm = jax.random.normal
    f32 = jnp.float32
    u_lam = jax.random.uniform(ks[10], (DEPTH, D_RNN), f32, 0.9, 0.999)
    sig_lam = u_lam ** (1.0 / LRU_C)
    lam = jnp.log(sig_lam) - jnp.log1p(-sig_lam)
    return {
        'x_prompt': nrm(ks[0], (BATCH, SEQ, D_MODEL), f32),
        'x_sample': nrm(ks[1], (DEC_BATCH, DEC_SEQ, D_MODEL), f32),
        'state_rnn_conv': nrm(ks[2], (DEPTH, DEC_BATCH, RNN_CONV_W - 1, D_RNN), f32),
        'state_rnn_h': 0.5 * nrm(ks[3], (DEPTH, DEC_BATCH, D_RNN), f32),
        'state_cm_conv': 0.5 * nrm(ks[4], (DEPTH, DEC_BATCH, CONV_W - 1, D_CONV), f32),
        'g_mix': 1.0 + 0.02 * nrm(ks[5], (DEPTH, D_MODEL), f32),
        'w_in': nrm(ks[6], (DEPTH, D_MODEL, IN_COLS), f32) * D_MODEL ** -0.5,
        'w_rconv': nrm(ks[7], (DEPTH, RNN_CONV_W, D_RNN), f32) * RNN_CONV_W ** -0.5,
        'b_rconv': 0.01 * nrm(ks[8], (DEPTH, D_RNN), f32),
        'w_r': nrm(ks[9], (DEPTH, RNN_HEADS, RNN_HEAD_DIM, RNN_HEAD_DIM), f32) * RNN_HEAD_DIM ** -0.5,
        'b_r': 0.01 * nrm(ks[11], (DEPTH, D_RNN), f32),
        'w_i': nrm(ks[12], (DEPTH, RNN_HEADS, RNN_HEAD_DIM, RNN_HEAD_DIM), f32) * RNN_HEAD_DIM ** -0.5,
        'b_i': 0.01 * nrm(ks[13], (DEPTH, D_RNN), f32),
        'lam': lam,
        'w_a': nrm(ks[14], (DEPTH, D_RNN, D_MODEL), f32) * D_RNN ** -0.5,
        'w_cconv': nrm(ks[15], (DEPTH, CONV_W, D_CONV), f32) * CONV_W ** -0.5,
        'b_cconv': 0.01 * nrm(ks[16], (DEPTH, D_CONV), f32),
        'ln_g': 1.0 + 0.02 * nrm(ks[17], (DEPTH, D_CONV), f32),
        'ln_b': 0.01 * nrm(ks[18], (DEPTH, D_CONV), f32),
        'w_b': nrm(ks[19], (DEPTH, D_CONV, D_MODEL), f32) * D_CONV ** -0.5,
        'w_out': nrm(ks[20], (DEPTH, D_MODEL, D_MODEL), f32) * D_MODEL ** -0.5,
        'g_ffn': 1.0 + 0.02 * nrm(ks[21], (DEPTH, D_MODEL), f32),
        'w_q': nrm(ks[22], (DEPTH, D_MODEL, PEER_HEADS * D_KEY), f32) * D_MODEL ** -0.5,
        'keys1': nrm(ks[23], (DEPTH, PEER_HEADS, N_KEYS, D_HALF), f32) * D_HALF ** -0.5,
        'keys2': nrm(ks[24], (DEPTH, PEER_HEADS, N_KEYS, D_HALF), f32) * D_HALF ** -0.5,
        'u_tab': nrm(ks[25], (DEPTH, N_EXPERTS, D_MODEL), f32) * D_MODEL ** -0.5,
        'v_tab': 0.25 * nrm(ks[26], (DEPTH, N_EXPERTS, D_MODEL), f32),
        'g_final': 1.0 + 0.02 * nrm(ks[27], (D_MODEL,), f32),
    }

def reference(x_prompt, x_sample, state_rnn_conv, state_rnn_h, state_cm_conv,
              g_mix, w_in, w_rconv, b_rconv, w_r, b_r, w_i, b_i, lam, w_a,
              w_cconv, b_cconv, ln_g, ln_b, w_b, w_out, g_ffn, w_q, keys1, keys2,
              u_tab, v_tab, g_final):
    p = {'g_mix': g_mix, 'w_in': w_in, 'w_rconv': w_rconv, 'b_rconv': b_rconv,
         'w_r': w_r, 'b_r': b_r, 'w_i': w_i, 'b_i': b_i, 'lam': lam, 'w_a': w_a,
         'w_cconv': w_cconv, 'b_cconv': b_cconv, 'ln_g': ln_g, 'ln_b': ln_b, 'w_b': w_b,
         'w_out': w_out, 'g_ffn': g_ffn, 'w_q': w_q, 'keys1': keys1, 'keys2': keys2,
         'u_tab': u_tab, 'v_tab': v_tab, 'g_final': g_final}
    bp = x_prompt.shape[0]
    dt = x_prompt.dtype
    p_rc0 = jnp.zeros((DEPTH, bp, RNN_CONV_W - 1, D_RNN), dt)
    p_h0 = jnp.zeros((DEPTH, bp, D_RNN), dt)
    p_cc0 = jnp.zeros((DEPTH, bp, CONV_W - 1, D_CONV), dt)
    y_prompt, p_rc, p_h, p_cc = _trunk(x_prompt, p_rc0, p_h0, p_cc0, p)
    y_sample, s_rc, s_h, s_cc = _trunk(x_sample, state_rnn_conv, state_rnn_h, state_cm_conv, p)
    return (y_prompt, y_sample, p_rc, p_h, p_cc, s_rc, s_h, s_cc)


_drawn_inputs = setup_inputs


def setup_inputs(seed=0):
    import zlib

    import numpy as np

    out = dict(_drawn_inputs(seed))
    spreads = {}
    factors = {'b_r': 21.518,
     'b_i': 8.0,
     'b_cconv': 4.781,
     'ln_g': 4.267,
     'ln_b': 7.125,
     'g_ffn': 3.164,
     'g_final': 7.938}
    for name, (base, spread) in spreads.items():
        noise = np.random.default_rng([zlib.crc32(name.encode()), seed]).standard_normal(out[name].shape)
        drawn = base * np.exp(spread * noise) if base else spread * noise
        out[name] = __import__('jax').numpy.asarray(drawn.astype(out[name].dtype))
    for name, factor in factors.items():
        out[name] = (out[name] * factor).astype(out[name].dtype)
    return out
```

```python
import concourse.bass as bass
from concourse import mybir
from contextlib import ExitStack

F32 = mybir.dt.float32
I32 = mybir.dt.int32
U32 = mybir.dt.uint32
ALU = mybir.AluOpType
ACT = mybir.ActivationFunctionType
AX = mybir.AxisListType

P = 128
D = 2048
DC = D // P
CH = 1024
CC = CH // P
TP = 512
NB, NS = 8, 4
TS = NB * NS
T = TP + TS
TH = T // 2
TX = TP + P
NT = TX // P
RW, CW = 4, 31
RPAD = RW - 1 + NS
CPAD = CW - 1 + NS
RFLAT = RW - 1 + TP + NB * RPAD
CFLAT = CW - 1 + TP + NB * CPAD
SCAN = TP + NB * (NS + 1)
NK = 128
HEADS = 8
TOPK = 16
UNITS = 4 * HEADS + 2
SLOTS = 4
EPS = 1e-6
LRU_C = 8.0
LOW = -3.0e38

R_WR, R_BR, R_BRG, R_BIG, R_LAM = 0, 4, 5, 6, 7
R_WC, R_BC, R_LNG, R_LNB, R_GM = 8, 39, 40, 41, 42
R_SRC, R_SH, R_N = 44, 68, 76
E_RCP, E_CCP, E_HP, E_RCS, E_CCS, E_HS, E_N = 0, 3, 33, 34, 58, 90, 98


class Steps:

    def __init__(self, eng, sem):
        self.eng, self.sem, self.base, self.n = eng, sem, 0, 0

    def mark(self, ins):
        ins.then_inc(self.sem, 1)
        self.n += 1

    def link(self, ins, alone=False):
        self.mark(ins)
        self.eng.wait_ge(self.sem, self.base + self.n)
        if alone:
            part(self.eng)

    def enter(self, i, per):
        self.start, self.per = self.base + self.n, per
        self.base, self.n = i * per + self.start, 0

    def leave(self, trips):
        assert self.n == self.per, (self.n, self.per)
        self.base, self.n = self.start + trips * self.per, 0


def part(eng):
    eng.nop(nofuse=True)


def hybrid_step(nc, x_prompt, x_sample, state_rnn_conv, state_rnn_h, state_cm_conv, g_mix, w_in,
                w_rconv, b_rconv, w_r, b_r, w_i, b_i, lam, w_a, w_cconv, b_cconv, ln_g, ln_b, w_b,
                w_out, g_ffn, w_q, keys1, keys2, u_tab, v_tab, g_final,
                y_prompt, y_sample, rc_p, h_p, cc_p, rc_s, h_s, cc_s):
    w_in_v = w_in.rearrange("l (k p) n -> p (l k) n", p=P)
    w_a_v = w_a.rearrange("l (k p) n -> p (l k) n", p=P)
    w_b_v = w_b.rearrange("l (k p) n -> p (l k) n", p=P)
    w_out_v = w_out.rearrange("l (k p) n -> p (l k) n", p=P)
    w_q_v = w_q.rearrange("l (k p) n -> p (l k) n", p=P)
    w_r_v = w_r.rearrange("l h i j -> i (l h) j")
    w_i_v = w_i.rearrange("l h i j -> i (l h) j")
    u_rows = u_tab.rearrange("l e d -> (l e) d")
    v_rows = v_tab.rearrange("l e d -> (l e) d")
    xs_rows = x_sample.rearrange("b s d -> (b s) d")

    with ExitStack() as ctx:
        def sb(name, n, dt=F32):
            return ctx.enter_context(nc.sbuf_tensor(name, [P, n], dt))

        def sem(name):
            return ctx.enter_context(nc.semaphore(name))

        res = sb("res", NT * D)
        reg_c = sb("reg_c", NT * D)
        reg_d = sb("reg_d", DC * T)
        reg_b = sb("reg_b", DC * T + 4 * D)
        reg_f = sb("reg_f", 2048)
        reg_k = sb("reg_k", 2048)
        xt = res[:, :].rearrange("p (t d) -> p t d", d=D)
        xn = reg_c[:, :].rearrange("p (t d) -> p t d", d=D)
        ha = reg_c[:, 0:CC * T].rearrange("p (c t) -> p c t", t=T)
        dc = reg_c[:, CC * T:2 * CC * T].rearrange("p (c t) -> p c t", t=T)
        ex = reg_c[:, 2 * CC * T:2 * CC * T + CC * E_N].rearrange("p (c e) -> p c e", e=E_N)
        gffn = xn[:, NT - 1, :]
        gfin = xn[:, 0, :]
        xnT = reg_b[:, 0:DC * T].rearrange("p (k t) -> p k t", t=T)
        wslot = [reg_b[:, DC * T + s * D:DC * T + (s + 1) * D].rearrange("p (k n) -> p k n", n=P)
                 for s in range(4)]
        ubuf = [reg_b[:, s * D:(s + 1) * D] for s in range(SLOTS)]
        vbuf = [reg_b[:, DC * T + s * D:DC * T + (s + 1) * D] for s in range(SLOTS)]
        merged = reg_d[:, :].rearrange("p (m t) -> p m t", t=T)
        sc = reg_d[:, 0:UNITS * 2 * NK].rearrange("p (u s k) -> p u s k", s=2, k=NK)
        keysT = reg_k[:, :].rearrange("p (s h k) -> p s h k", s=2, h=HEADS)
        diag = reg_k[:, :].rearrange("p (k m) -> p k m", m=P)

        rows = reg_d[:, 0:CH]
        cmrows = reg_d[:, CH:3 * CH].rearrange("p (a n) -> p a n", a=2)
        krows = reg_d[:, 3 * CH:5 * CH].rearrange("p (s h d) -> p s h d", s=2, h=HEADS)

        at = [0]

        def cut(n):
            at[0] += n
            return reg_d[:, at[0] - n:at[0]]

        yg, rg, ig, th, t1, t2, cg = (cut(T) for _ in range(7))
        xcv, bb, hh, acc31 = cut(576), cut(SCAN), cut(SCAN), cut(816)
        assert at[0] >= 5 * CH
        xrpad, glupad, aa = cut(576), cut(816), cut(SCAN)
        assert at[0] <= DC * T
        cmT = reg_f[:, 0:CC * NB * (CW - 1)].rearrange("p (c e) -> p c e", c=CC)
        sga, sgb = reg_f[:, 0:T], reg_f[:, T:2 * T]
        blockT = [reg_f[:, j * TX:(j + 1) * TX] for j in range(2)]

        sel_t = sb("sel_t", 2 * P)
        ones = sb("ones", P)
        par_t = sb("par_t", CC * R_N)
        gw_t = sb("gw_t", 2 * P)
        rows_out = sb("rows_out", CH)
        small = sb("small", 96)
        sel = sel_t[:, :].rearrange("p (s m) -> p s m", s=2)
        ident = sel[:, 0, :]
        par = par_t[:, :].rearrange("p (c r) -> p c r", r=R_N)
        gw = gw_t[:, :].rearrange("p (s j) -> p s j", s=2)
        cneg, cpos = small[:, 0:8], small[:, 8:16]
        sp_a, sp_b, sp_c, sp_d = (small[:, 16 + 8 * j:24 + 8 * j] for j in range(4))
        ssq, rstd, eps = small[:, 48:53], small[:, 56:61], small[:, 64:65]
        mask = small[:, 68:72]

        at2 = [0]

        def cutf(n, dt=None):
            at2[0] += n
            v = reg_f[:, at2[0] - n:at2[0]]
            return v if dt is None else v.bitcast(dt)

        scur = cutf(256).rearrange("p (s k) -> p s k", s=2)
        swork = cutf(256).rearrange("p (s k) -> p s k", s=2)
        cand, cwork, eq = cutf(256), cutf(256), cutf(512)
        top = cutf(32).rearrange("p (s k) -> p s k", s=2)
        topi = cutf(32, U32).rearrange("p (s k) -> p s k", s=2)
        topf = cutf(32).rearrange("p (s k) -> p s k", s=2)
        sv, si = cutf(16), cutf(16, U32)
        ab = cutf(32, U32).rearrange("p (s k) -> p s k", s=2)
        abf, ei = cutf(32), cutf(32).rearrange("p (s k) -> p s k", s=2)
        iota16 = cutf(16)
        idx_u = [cutf(16, I32) for _ in range(2)]
        idx_v = [cutf(16, I32) for _ in range(2)]
        dots = [cutf(16) for _ in range(2)]
        gate = [cutf(16) for _ in range(2)]
        wts = [cutf(16) for _ in range(2)]
        gel, ex16, nmax, esum, ersum = cutf(16), cutf(16), cutf(1), cutf(1), cutf(1)
        assert at2[0] <= 2048
        iota_s = sb("iota_s", 16)

        ps = ctx.enter_context(nc.psum_tensor("ps", [P, 4, 1024], F32))
        halves = [ps[:, j, :].rearrange("p (a n) -> p a n", a=2)[:, :, 0:TH] for j in range(4)]
        acc = ps[:, 0:2, :].rearrange("p a n -> p (a n)")

        const_ready = sem("const_ready")
        rows_in, keys_in = sem("rows_in"), sem("keys_in")
        x_in = [sem(f"x_in{t}") for t in range(NT)]
        ssq_ready, rms_sqrt, xn_ready = sem("ssq_ready"), sem("rms_sqrt"), sem("xn_ready")
        stagedT, staged_read = sem("stagedT"), sem("staged_read")
        xT_done, xT_act, xT_dve = sem("xT_done"), sem("xT_act"), sem("xT_dve")
        exp_lam, lam_abs, lru_ready = sem("exp_lam"), sem("lam_abs"), sem("lru_ready")
        w_landed = [sem(f"w_landed{s}") for s in range(4)]
        gw_landed = sem("gw_landed")
        xr_done, yr_done, ca_done, cb_done = sem("xr_done"), sem("yr_done"), sem("ca_done"), sem("cb_done")
        rgate_done, igate_done = sem("rgate_done"), sem("igate_done")
        xr_padded, yg_ready, xcv_ready = sem("xr_padded"), sem("yg_ready"), sem("xcv_ready")
        rg_ready, ig_ready, decay_ready = sem("rg_ready"), sem("ig_ready"), sem("decay_ready")
        beta2_ready, beta_ready, ha_ready = sem("beta2_ready"), sem("beta_ready"), sem("ha_ready")
        cg_ready, glu_ready, dc_ready = sem("cg_ready"), sem("glu_ready"), sem("dc_ready")
        mean_done, mean_read, centered = sem("mean_done"), sem("mean_read"), sem("centered")
        sq_ready, sq_used, sd_ready = sem("sq_ready"), sem("sq_used"), sem("sd_ready")
        scaled, silu_ready = sem("scaled"), sem("silu_ready")
        exT_done, exT_read = sem("exT_done"), sem("exT_read")
        ga_done, gb_done, ba_done, bb_done = sem("ga_done"), sem("gb_done"), sem("ba_done"), sem("bb_done")
        sga_ready, sgb_ready = sem("sga_ready"), sem("sgb_ready")
        a_gated, merged_ready = sem("a_gated"), sem("merged_ready")
        out_done = sem("out_done")
        outT_ready = [sem(f"outT_ready{j}") for j in range(2)]
        outX_done = [sem(f"outX_done{j}") for j in range(2)]
        x1_ready = [sem(f"x1_ready{j}") for j in range(2)]
        gffn_in, gfin_in = sem("gffn_in"), sem("gfin_in")
        q_done = sem("q_done")
        qT_ready = [sem(f"qT_ready{j}") for j in range(2)]
        s_done = [sem(f"s_done{j}") for j in range(2)]
        s_read = [sem(f"s_read{j}") for j in range(2)]
        s4_read = [sem(f"s4_read{j}") for j in range(2)]
        sc_zero = sem("sc_zero")
        u_landed = [sem(f"u_landed{s}") for s in range(SLOTS)]
        v_landed = [sem(f"v_landed{s}") for s in range(SLOTS)]
        staged_scores, top_ready, exp_ready = sem("staged_scores"), sem("top_ready"), sem("exp_ready")
        routed, idx_set, idx_copied = sem("routed"), sem("idx_set"), sem("idx_copied")
        dot_done, gelu_ready, w_ready = sem("dot_done"), sem("gelu_ready"), sem("w_ready")
        diag_ready, v_used, acc_read = sem("diag_ready"), sem("v_used"), sem("acc_read")
        y_ready = sem("y_ready")
        out_p, out_a = sem("out_p"), sem("out_a")
        dve_step, pool_step = sem("dve_step"), sem("pool_step")

        pe_counts = [xr_done, yr_done, ca_done, cb_done, igate_done, ga_done, gb_done, ba_done, bb_done,
                     *outX_done, *s_done]
        act_counts = [rg_ready, ig_ready, cg_ready, sga_ready, sgb_ready, diag_ready, *outT_ready,
                      *qT_ready, *s_read]
        dve_counts = [glu_ready, ha_ready, xcv_ready, merged_ready, a_gated, acc_read, *x1_ready, *s4_read]

        block = ctx.enter_context(nc.Block())

        @block.sync
        def _(sp):
            for t in range(NT - 1):
                sp.dma_start(xt[:, t, :], x_prompt[0, t * P:(t + 1) * P, :]).then_inc(x_in[t], 16)
            for g in range(4):
                sp.dma_start(xt[g * TS:(g + 1) * TS, NT - 1, :], xs_rows).then_inc(x_in[NT - 1], 16)

            with sp.Fori(0, CC) as c:
                for s, (col, used) in enumerate([(0, xr_done), (CH, yr_done), (2 * CH, ca_done),
                                                 (3 * CH, cb_done)]):
                    sp.wait_ge(used, c + 1)
                    sp.dma_start(wslot[s], w_in_v[:, :, bass.ds(c * P + col, P)]).then_inc(w_landed[s], 16)
                    if s == 1:
                        sp.wait_ge(igate_done, c + 1)
                        sp.dma_start(gw[:, 0, :], w_r_v[:, c, :]).then_inc(gw_landed, 16)
                        sp.dma_start(gw[:, 1, :], w_i_v[:, c, :]).then_inc(gw_landed, 16)
            for s, used in enumerate((xr_done, yr_done, ca_done, cb_done)):
                sp.wait_ge(used, CC + 1)
            with sp.Fori(0, DC) as m:
                sp.wait_ge(ga_done, m + 1)
                sp.dma_start(wslot[0], w_in_v[:, :, bass.ds(m * P + 4 * CH, P)]).then_inc(w_landed[0], 16)
                sp.wait_ge(gb_done, m + 1)
                sp.dma_start(wslot[1], w_in_v[:, :, bass.ds(m * P + 4 * CH + D, P)]).then_inc(w_landed[1], 16)
                sp.wait_ge(ba_done, m + 1)
                part(sp)
                sp.dma_start(wslot[2][:, 0:CC, :], w_a_v[:, :, bass.ds(m * P, P)]).then_inc(w_landed[2], 16)
                sp.wait_ge(bb_done, m + 1)
                sp.dma_start(wslot[3][:, 0:CC, :], w_b_v[:, :, bass.ds(m * P, P)]).then_inc(w_landed[3], 16)
            for used in (ga_done, gb_done, ba_done, bb_done):
                sp.wait_ge(used, DC + 1)
            for s in range(4):
                sp.dma_start(wslot[s], w_out_v[:, :, s * P:(s + 1) * P]).then_inc(w_landed[s], 16)
            with sp.Fori(0, 3) as i:
                for s in range(4):
                    sp.wait_ge(out_done, i * 4 + s + 1)
                    sp.dma_start(wslot[s], w_out_v[:, :, bass.ds(i * 4 * P + (s + 4) * P, P)]).then_inc(w_landed[s], 16)
            sp.dma_start(gffn, g_ffn.partition_broadcast(P)).then_inc(gffn_in, 16)
            for s in range(4):
                sp.wait_ge(out_done, 12 + s + 1)
                sp.dma_start(wslot[s], w_q_v[:, :, s * P:(s + 1) * P]).then_inc(w_landed[s], 16)
            with sp.Fori(0, 3) as i:
                for s in range(4):
                    sp.wait_ge(q_done, i * 4 + s + 1)
                    sp.dma_start(wslot[s], w_q_v[:, :, bass.ds(i * 4 * P + (s + 4) * P, P)]).then_inc(w_landed[s], 16)
            sp.wait_ge(dot_done, TOPK * HEADS)
            sp.dma_start(gfin, g_final.partition_broadcast(P)).then_inc(gfin_in, 16)
            for t in range(NT - 1):
                sp.wait_ge(y_ready, t + 1)
                sp.dma_start(y_prompt[0, t * P:(t + 1) * P, :], xt[:, t, :]).then_inc(out_p, 16)
            sp.wait_ge(y_ready, NT)
            sp.dma_start(y_sample.rearrange("b s d -> (b s) d"), xt[0:TS, NT - 1, :]).then_inc(out_p, 16)
            sp.wait_ge(out_p, 16 * NT)

        @block.gpsimd
        def _(pool):
            step = Steps(pool, pool_step)
            step.link(nc.gpsimd.memset(ones[:, :], 1.0))
            step.link(nc.gpsimd.memset(small[:, 64:65], EPS))
            step.link(nc.gpsimd.memset(mask, 0.0))
            step.link(nc.gpsimd.memset(sel_t[:, :], 0.0))
            step.link(nc.gpsimd.affine_select(out=ident, in_=ident, compare_op=ALU.not_equal, fill=1.0,
                                              base=0, pattern=[[-1, P]], channel_multiplier=1))
            for g in range(4):
                q = slice(g * TS, (g + 1) * TS)
                step.link(nc.gpsimd.memset(mask[q, g:g + 1], 1.0))
                step.link(nc.gpsimd.tensor_copy(sel[q, 1, 0:TS], ident[q, q]))
            step.link(nc.gpsimd.iota(iota_s[:, :], pattern=[[1, TOPK]], base=0, channel_multiplier=0,
                                     allow_small_or_imprecise_dtypes=True))
            step.link(nc.gpsimd.memset(xrpad[:, 0:RW - 1], 0.0))
            step.link(nc.gpsimd.memset(glupad[:, 0:CW - 1], 0.0))
            nc.gpsimd.memset(aa, 0.0).then_inc(const_ready, 1)

            def gather(rows_ap, slot, landed, idx, k):
                part(pool)
                pool.indirect_dma_start(out=slot, out_offset=None, in_=rows_ap,
                                        in_offset=bass.IndirectOffsetOnAxis(ap=idx[:, k:k + 1], axis=0)
                                        ).then_inc(landed, 16)

            def gather_unit(u, parity, u_side=True, v_side=True, u_fresh=False, v_fresh=False):
                if u_side:
                    pool.wait_ge(routed, u + 1)
                if v_side:
                    part(pool)
                    nc.gpsimd.tensor_copy(idx_v[1 - parity], idx_u[1 - parity]).then_inc(idx_copied, 1)
                    pool.wait_ge(idx_copied, u)
                for k in range(TOPK):
                    s = k % SLOTS
                    if u_side:
                        if not (u_fresh and k < SLOTS):
                            pool.wait_ge(dot_done, u * TOPK + (k - SLOTS + 1))
                        gather(u_rows, ubuf[s], u_landed[s], idx_u[parity], k)
                    if v_side:
                        if not (v_fresh and k < SLOTS):
                            pool.wait_ge(v_used, u * TOPK + (k - SLOTS + 1 - TOPK))
                        gather(v_rows, vbuf[s], v_landed[s], idx_v[1 - parity], k)

            pool.wait_ge(q_done, 2 * HEADS)
            gather_unit(0, 0, v_side=False, u_fresh=True)
            gather_unit(1, 1, v_fresh=True)
            with pool.Fori(1, UNITS // 2) as i:
                gather_unit(i * 2, 0)
                gather_unit(i * 2 + 1, 1)
            gather_unit(UNITS, 0, u_side=False)

        @block.scalar
        def _(act):
            for s in act_counts:
                act.sem_inc(s, 1)
            for r, src in [(R_WR, w_rconv[0]), (R_BR, b_rconv), (R_BRG, b_r), (R_BIG, b_i), (R_LAM, lam),
                           (R_WC, w_cconv[0]), (R_BC, b_cconv), (R_LNG, ln_g), (R_LNB, ln_b),
                           (R_GM, g_mix.rearrange("l (a n) -> (l a) n", n=CH)),
                           (R_SRC, state_rnn_conv.rearrange("l b j n -> (l b j) n")), (R_SH, state_rnn_h[0])]:
                act.dma_start(rows[r:r + src.shape[0], :], src).then_inc(rows_in, 16)
            cm = state_cm_conv.rearrange("l (a b) j n -> a (l b j) n", a=2)
            for a in range(2):
                act.dma_start(cmrows[0:NB * (CW - 1) // 2, a, :], cm[a]).then_inc(rows_in, 16)
            act.dma_start(krows[:, 0], keys1.rearrange("l h k d -> k (l h) d")).then_inc(keys_in, 16)
            act.dma_start(krows[:, 1], keys2.rearrange("l h k d -> k (l h) d")).then_inc(keys_in, 16)
            act.dma_start(cc_s[0, :, 0:CW - 1 - NS, :], state_cm_conv[0, :, NS:CW - 1, :]).then_inc(out_a, 16)

            def sum_squares(t, junk):
                nc.scalar.activation(junk, xt[:, t, :], ACT.Square, accum_out=ssq[:, t:t + 1]).then_inc(ssq_ready, 1)

            def root(n):
                act.wait_ge(ssq_ready, n * NT)
                nc.scalar.activation(rstd, ssq, ACT.Sqrt, bias=eps, scale=1.0 / D).then_inc(rms_sqrt, 1)

            act.wait_ge(const_ready, 1)
            for t in range(NT):
                act.wait_ge(x_in[t], 64 if t == NT - 1 else 16)
                sum_squares(t, xn[:, t, :])
            root(1)
            act.wait_ge(stagedT, 1)
            nc.scalar.activation(keysT[:, 0].rearrange("p h k -> p (h k)"), ps[:, 0, :], ACT.Copy).then_inc(staged_read, 1)
            act.wait_ge(stagedT, 2)
            nc.scalar.activation(keysT[:, 1].rearrange("p h k -> p (h k)"), ps[:, 1, :], ACT.Copy).then_inc(staged_read, 1)
            act.wait_ge(stagedT, 3)
            for b in range(2):
                last = nc.scalar.activation(par[:, 4 * b:4 * b + 4, :],
                                            ps[:, 2, 512 * b:512 * b + 4 * R_N].rearrange("p (c r) -> p c r", r=R_N),
                                            ACT.Copy)
            last.then_inc(staged_read, 1)
            for n, (j, base) in enumerate(((3, 0), (0, 4))):
                act.wait_ge(stagedT, 4 + n)
                for b in range(2):
                    last = nc.scalar.activation(cmT[:, base + 2 * b:base + 2 * b + 2, :],
                                                ps[:, j, 512 * b:512 * b + 480].rearrange("p (c r) -> p c r", r=240),
                                                ACT.Copy)
                last.then_inc(staged_read, 1)
            act.wait_ge(lam_abs, 1)
            nc.scalar.activation(sp_b, sp_a, ACT.Exp, scale=-1.0).then_inc(exp_lam, 1)
            act.wait_ge(staged_read, 5)
            for k in range(0, DC, 2):
                act.wait_ge(xT_done, k + 1)
                nc.scalar.activation(xnT[:, k, :], ps[:, k % 4, 0:T], ACT.Copy,
                                     scale=par[:, k % CC, R_GM + k // CC:R_GM + k // CC + 1]).then_inc(xT_act, 1)

            act.wait_ge(lru_ready, 1)
            xr_s = xrpad[:, RW - 1 + TP:RFLAT].rearrange("p (b j) -> p b j", j=RPAD)
            aa_s = aa[:, TP:SCAN].rearrange("p (b j) -> p b j", j=NS + 1)
            with act.Fori(0, CC) as c:
                act.wait_ge(xr_done, c + 2)
                act.wait_ge(xcv_ready, c + 1)
                nc.scalar.activation(xrpad[:, RW - 1:RW - 1 + TH], halves[0][:, 0, :], ACT.Copy)
                nc.scalar.activation(xrpad[:, RW - 1 + TH:RW - 1 + TP], halves[0][:, 1, 0:TP - TH], ACT.Copy)
                nc.scalar.activation(xr_s[:, :, RW - 1:RPAD],
                                     halves[0][:, 1, TP - TH:TH].rearrange("p (b s) -> p b s", s=NS), ACT.Copy)
                nc.scalar.activation(xr_s[:, :, 0:RW - 1],
                                     par[:, c, R_SRC:R_SH].rearrange("p (b j) -> p b j", j=RW - 1),
                                     ACT.Copy).then_inc(xr_padded, 1)
                act.wait_ge(yr_done, c + 2)
                act.wait_ge(ha_ready, c + 1)
                nc.scalar.activation(yg.rearrange("p (a n) -> p a n", a=2), halves[1], ACT.Gelu_apprx_tanh).then_inc(yg_ready, 1)
                act.wait_ge(rgate_done, c + 1)
                nc.scalar.activation(rg, ps[:, 0, 0:T], ACT.Sigmoid, bias=par[:, c, R_BRG:R_BRG + 1]).then_inc(rg_ready, 1)
                act.wait_ge(igate_done, c + 2)
                nc.scalar.activation(ig, ps[:, 1, 0:T], ACT.Sigmoid, bias=par[:, c, R_BIG:R_BIG + 1]).then_inc(ig_ready, 1)
                act.wait_ge(rg_ready, c + 2)
                nc.scalar.activation(aa[:, 0:TP], rg[:, 0:TP], ACT.Exp, scale=cneg[:, bass.ds(c, 1)])
                nc.scalar.activation(aa_s[:, :, 1:NS + 1], rg[:, TP:T].rearrange("p (b s) -> p b s", s=NS),
                                     ACT.Exp, scale=cneg[:, bass.ds(c, 1)])
                nc.scalar.activation(th, rg, ACT.Tanh, scale=cpos[:, bass.ds(c, 1)]).then_inc(decay_ready, 1)
                act.wait_ge(beta2_ready, c + 1)
                nc.scalar.activation(t2, t1, ACT.Sqrt).then_inc(beta_ready, 1)
                act.wait_ge(cb_done, c + 2)
                act.wait_ge(glu_ready, c + 1)
                nc.scalar.activation(cg.rearrange("p (a n) -> p a n", a=2), halves[3], ACT.Sigmoid).then_inc(cg_ready, 1)

            sqb = (th, t2)
            for c in range(CC):
                act.wait_ge(centered, c + 1)
                if c >= 2:
                    act.wait_ge(sq_used, c - 1)
                nc.scalar.activation(sqb[c % 2], dc[:, c, :], ACT.Square).then_inc(sq_ready, 1)
            act.wait_ge(sq_used, CC)
            nc.scalar.activation(rg.rearrange("p (a n) -> p a n", a=2), halves[1], ACT.Sqrt, bias=eps,
                                 scale=1.0 / CH).then_inc(sd_ready, 1)
            act.wait_ge(exT_done, 1)
            nc.scalar.activation(rows_out[0:E_N, :], ps[0:E_N, 2, :], ACT.Copy).then_inc(exT_read, 1)
            for c in range(CC):
                act.wait_ge(scaled, c + 1)
                nc.scalar.activation(dc[:, c, :], dc[:, c, :], ACT.Silu, scale=par[:, c, R_LNG:R_LNG + 1],
                                     bias=par[:, c, R_LNB:R_LNB + 1]).then_inc(silu_ready, 1)
            act.wait_ge(exT_read, 1)
            for dst, r, n in [(rc_p.rearrange("l b j n -> (l b j) n"), E_RCP, 3),
                              (cc_p.rearrange("l b j n -> (l b j) n"), E_CCP, 30),
                              (h_p.rearrange("l b n -> (l b) n"), E_HP, 1),
                              (rc_s.rearrange("l b j n -> (l b j) n"), E_RCS, 24),
                              (h_s.rearrange("l b n -> (l b) n"), E_HS, 8)]:
                act.dma_start(dst, rows_out[r:r + n, :]).then_inc(out_a, 16)
            for b in range(NB):
                act.dma_start(cc_s[0, b, CW - 1 - NS:CW - 1, :],
                              rows_out[E_CCS + b * NS:E_CCS + (b + 1) * NS, :]).then_inc(out_a, 16)

            with act.Fori(0, DC) as m:
                act.wait_ge(ga_done, m + 2)
                act.wait_ge(merged_ready, m + 1)
                nc.scalar.activation(sga.rearrange("p (a n) -> p a n", a=2), halves[0], ACT.Sigmoid).then_inc(sga_ready, 1)
                act.wait_ge(gb_done, m + 2)
                nc.scalar.activation(sgb.rearrange("p (a n) -> p a n", a=2), halves[1], ACT.Sigmoid).then_inc(sgb_ready, 1)

            def widen(j):
                nc.scalar.activation(blockT[j][:, 0:TH], halves[j][:, 0, :], ACT.Copy)
                nc.scalar.activation(blockT[j][:, TH:TP], halves[j][:, 1, 0:TP - TH], ACT.Copy)
                return nc.scalar.activation(
                    blockT[j][:, TP:TX].rearrange("p (g t) -> p g t", g=4),
                    halves[j][:, 1, TP - TH:TH].unsqueeze(1).to_broadcast([P, 4, TS]), ACT.Copy)

            act.wait_ge(merged_ready, DC + 1)
            with act.Fori(0, 4) as i:
                for j in range(4):
                    act.wait_ge(out_done, i * 4 + j + 1)
                    act.wait_ge(outX_done[j % 2], i * 2 + j // 2 + 1)
                    widen(j % 2).then_inc(outT_ready[j % 2], 1)

            for j in range(2):
                act.wait_ge(x1_ready[j], DC // 2 + 1)
            for t in range(NT):
                act.wait_ge(ssq_ready, NT + t)
                sum_squares(t, reg_d[:, 0:D])
            root(2)
            for k in range(0, DC, 2):
                act.wait_ge(xT_done, DC + k + 1)
                nc.scalar.activation(xnT[:, k, :], ps[:, k % 4, 0:T], ACT.Copy).then_inc(xT_act, 1)

            sc32 = sc[:, 0:4 * HEADS].rearrange("p (t h) s k -> p t h s k", h=HEADS)
            with act.Fori(0, 4) as i:
                def query(j):
                    act.wait_ge(q_done, i * 4 + j + 1)
                    act.wait_ge(s_done[j % 2], i * 2 + j // 2 + 1)
                    widen(j % 2).then_inc(qT_ready[j % 2], 1)

                def scores(j):
                    act.wait_ge(s_done[j % 2], i * 2 + j // 2 + 2)
                    nc.scalar.activation(sc32[:, :, i * 2 + j // 2, j % 2, :],
                                         ps[:, 2 + j % 2, 0:4 * NK].rearrange("p (t k) -> p t k", k=NK),
                                         ACT.Copy).then_inc(s_read[j % 2], 1)

                query(0)
                query(1)
                scores(0)
                query(2)
                scores(1)
                query(3)
                scores(2)
                scores(3)

            def stage_scores(u):
                act.wait_ge(routed, u)
                part(act)
                nc.scalar.activation(scur, sc[:, u], ACT.Copy).then_inc(staged_scores, 1)

            def softmax_exp(u):
                act.wait_ge(top_ready, u + 1)
                nc.scalar.activation(ex16, sv, ACT.Exp, bias=nmax, accum_out=esum).then_inc(exp_ready, 1)

            def weigh(u, par_u, first=False):
                act.wait_ge(dot_done, (u + 1) * TOPK)
                act.wait_ge(w_ready, u)
                nc.scalar.activation(gel, dots[par_u], ACT.Gelu_apprx_tanh).then_inc(gelu_ready, 1)
                act.wait_ge(w_ready, u + 1)
                for k in range(TOPK):
                    if not first:
                        act.wait_ge(v_used, u * TOPK + (k - TOPK + 1))
                    part(act)
                    nc.scalar.activation(diag[:, k, :], sel[:, u >> 5, :], ACT.Copy,
                                         scale=wts[par_u][:, k:k + 1]).then_inc(diag_ready, 1)

            for j in range(2):
                act.wait_ge(s4_read[j], HEADS + 1)
            for j in range(2):
                act.wait_ge(s_read[j], HEADS + 1)
            stage_scores(0)
            softmax_exp(0)
            stage_scores(1)
            softmax_exp(1)
            weigh(0, 0, first=True)
            with act.Fori(0, (UNITS - 2) // 2) as i:
                for n in (1, 2):
                    stage_scores(i * 2 + (n + 1))
                    softmax_exp(i * 2 + (n + 1))
                    weigh(i * 2 + n, n % 2)
            weigh(UNITS - 1, (UNITS - 1) % 2)

            act.wait_ge(acc_read, UNITS + 1)
            for t in range(NT):
                act.wait_ge(ssq_ready, 2 * NT + t)
                sum_squares(t, reg_d[:, 0:D])
            root(3)
            act.wait_ge(out_a, 16 * (6 + NB))

        @block.vector
        def _(dve):
            for s in dve_counts:
                dve.sem_inc(s, 1)
            step = Steps(dve, dve_step)
            mark, link = step.mark, step.link
            stt, tt, ts_ = nc.vector.scalar_tensor_tensor, nc.vector.tensor_tensor, nc.vector.tensor_scalar

            dve.wait_ge(rms_sqrt, 1)
            link(nc.vector.reciprocal(rstd, rstd))
            for t in range(NT):
                ts_(xn[:, t, :], xt[:, t, :], rstd[:, t:t + 1], None, ALU.mult).then_inc(xn_ready, 1)

            dve.wait_ge(staged_read, 3)
            lam_c = par[:, :, R_LAM]
            stt(out=sp_a, in0=lam_c, scalar=-1.0, in1=lam_c, op0=ALU.mult, op1=ALU.max).then_inc(lam_abs, 1)
            dve.wait_ge(exp_lam, 1)
            link(ts_(sp_c, sp_b, 2.0, None, ALU.add))
            link(nc.vector.reciprocal(sp_c, sp_c))
            link(tt(sp_b, sp_b, sp_c, ALU.mult))
            link(tt(sp_c, sp_b, sp_b, ALU.mult))
            link(ts_(sp_d, sp_c, 1.0 / 17, None, ALU.mult))
            for n in (15, 13, 11, 9, 7, 5, 3):
                link(stt(out=sp_d, in0=sp_d, scalar=1.0 / n, in1=sp_c, op0=ALU.add, op1=ALU.mult))
            link(stt(out=sp_d, in0=sp_d, scalar=1.0, in1=sp_b, op0=ALU.add, op1=ALU.mult))
            link(ts_(sp_a, lam_c, -1.0, 0.0, ALU.mult, ALU.max))
            link(stt(out=sp_d, in0=sp_d, scalar=2.0, in1=sp_a, op0=ALU.mult, op1=ALU.add))
            link(ts_(cpos, sp_d, LRU_C, None, ALU.mult))
            ts_(cneg, sp_d, -LRU_C, None, ALU.mult).then_inc(lru_ready, 1)
            dve.wait_ge(lru_ready, 1)
            for k in range(1, DC, 2):
                dve.wait_ge(xT_done, k + 1)
                ts_(xnT[:, k, :], ps[:, k % 4, 0:T],
                    par[:, k % CC, R_GM + k // CC:R_GM + k // CC + 1], None, ALU.mult).then_inc(xT_dve, 1)

            xr_s = xrpad[:, RW - 1 + TP:RFLAT].rearrange("p (b j) -> p b j", j=RPAD)
            gl_s = glupad[:, CW - 1 + TP:CFLAT].rearrange("p (b j) -> p b j", j=CPAD)
            aa_s = aa[:, TP:SCAN].rearrange("p (b j) -> p b j", j=NS + 1)
            bb_s = bb[:, TP:SCAN].rearrange("p (b j) -> p b j", j=NS + 1)
            hh_s = hh[:, TP:SCAN].rearrange("p (b j) -> p b j", j=NS + 1)
            xc_s = xcv[:, TP + RW - 1:TP + RW - 1 + NB * RPAD].rearrange("p (b j) -> p b j", j=RPAD)[:, :, 0:NS]

            def bs(ap):
                return ap.rearrange("p (b s) -> p b s", s=NS)

            n4, n31 = RFLAT - RW + 1, CFLAT - CW + 1
            ac_s = acc31[:, TP + CW - 1:CFLAT].rearrange("p (b j) -> p b j", j=CPAD)[:, :, 0:NS]
            dve.wait_ge(const_ready, 1)
            with dve.Fori(0, CC) as c:
                step.enter(c, 52)
                dve.wait_ge(xr_padded, c + 1)
                mark(nc.vector.tensor_copy(ex[:, c, E_RCP:E_RCP + 3], xrpad[:, TP:TP + RW - 1]))
                mark(nc.vector.tensor_copy(ex[:, c, E_RCS:E_RCS + 24].rearrange("p (b j) -> p b j", j=3),
                                           xr_s[:, :, NS:RPAD]))
                dve.wait_ge(igate_done, c + 1)
                link(ts_(xcv[:, 0:n4], xrpad[:, 0:n4], par[:, c, R_WR:R_WR + 1], par[:, c, R_BR:R_BR + 1],
                         ALU.mult, ALU.add))
                for k in range(1, RW):
                    ins = stt(out=xcv[:, 0:n4], in0=xrpad[:, k:k + n4], scalar=par[:, c, R_WR + k:R_WR + k + 1],
                              in1=xcv[:, 0:n4], op0=ALU.mult, op1=ALU.add)
                    if k < RW - 1:
                        link(ins)
                ins.then_inc(xcv_ready, 1)
                dve.wait_ge(decay_ready, c + 1)
                mark(tt(t1[:, 0:TP], aa[:, 0:TP], aa[:, 0:TP], ALU.mult))
                link(tt(bs(t1[:, TP:T]), aa_s[:, :, 1:NS + 1], aa_s[:, :, 1:NS + 1], ALU.mult))
                stt(out=t1, in0=t1, scalar=1.0, in1=th, op0=ALU.add, op1=ALU.mult).then_inc(beta2_ready, 1)
                dve.wait_ge(xcv_ready, c + 2)
                dve.wait_ge(ig_ready, c + 2)
                mark(tt(bb[:, 0:TP], ig[:, 0:TP], xcv[:, 0:TP], ALU.mult))
                mark(tt(bb_s[:, :, 1:NS + 1], bs(ig[:, TP:T]), xc_s, ALU.mult))
                link(nc.vector.tensor_copy(bb_s[:, :, 0], par[:, c, R_SH:R_N]))
                dve.wait_ge(beta_ready, c + 1)
                mark(tt(bb[:, 0:TP], bb[:, 0:TP], t2[:, 0:TP], ALU.mult))
                link(tt(bb_s[:, :, 1:NS + 1], bb_s[:, :, 1:NS + 1], bs(t2[:, TP:T]), ALU.mult))
                link(nc.vector.tensor_tensor_scan(out=hh, data0=aa, data1=bb, initial=0.0, op0=ALU.mult, op1=ALU.add))
                mark(nc.vector.tensor_copy(ex[:, c, E_HP:E_HP + 1], hh[:, TP - 1:TP]))
                mark(nc.vector.tensor_copy(ex[:, c, E_HS:E_N], hh_s[:, :, NS]))
                dve.wait_ge(yg_ready, c + 1)
                mark(tt(ha[:, c, 0:TP], hh[:, 0:TP], yg[:, 0:TP], ALU.mult))
                tt(bs(ha[:, c, TP:T]), hh_s[:, :, 1:NS + 1], bs(yg[:, TP:T]), ALU.mult).then_inc(ha_ready, 1)
                dve.wait_ge(ca_done, c + 2)
                dve.wait_ge(cg_ready, c + 2)
                mark(nc.vector.tensor_copy(gl_s[:, :, 0:CW - 1], cmT[:, c, :].rearrange("p (b j) -> p b j", j=CW - 1)))
                mark(tt(glupad[:, CW - 1:CW - 1 + TH], halves[2][:, 0, :], cg[:, 0:TH], ALU.mult))
                mark(tt(glupad[:, CW - 1 + TH:CW - 1 + TP], halves[2][:, 1, 0:TP - TH], cg[:, TH:TP], ALU.mult))
                tt(gl_s[:, :, CW - 1:CPAD], bs(halves[2][:, 1, TP - TH:TH]), bs(cg[:, TP:T]), ALU.mult).then_inc(glu_ready, 1)
                dve.wait_ge(glu_ready, c + 2)
                mark(nc.vector.tensor_copy(ex[:, c, E_CCP:E_CCP + 30], glupad[:, TP:TP + CW - 1]))
                mark(nc.vector.tensor_copy(ex[:, c, E_CCS:E_CCS + TS].rearrange("p (b j) -> p b j", j=NS),
                                           gl_s[:, :, CW - 1:CPAD]))
                link(ts_(acc31[:, 0:n31], glupad[:, 0:n31], par[:, c, R_WC:R_WC + 1], par[:, c, R_BC:R_BC + 1],
                         ALU.mult, ALU.add))
                for k in range(1, CW - 1):
                    link(stt(out=acc31[:, 0:n31], in0=glupad[:, k:k + n31],
                             scalar=par[:, c, R_WC + k:R_WC + k + 1], in1=acc31[:, 0:n31],
                             op0=ALU.mult, op1=ALU.add))
                k = CW - 1
                w_k = par[:, c, R_WC + k:R_WC + k + 1]
                mark(stt(out=dc[:, c, 0:TP], in0=glupad[:, k:k + TP], scalar=w_k, in1=acc31[:, 0:TP],
                         op0=ALU.mult, op1=ALU.add))
                stt(out=bs(dc[:, c, TP:T]), in0=gl_s[:, :, k:CPAD], scalar=w_k, in1=ac_s,
                    op0=ALU.mult, op1=ALU.add).then_inc(dc_ready, 1)
                step.leave(CC)

            def two(ap):
                return ap.rearrange("p (a n) -> p a n", a=2)

            dve.wait_ge(mean_done, 1)
            ts_(two(t1), halves[0], -1.0 / CH, None, ALU.mult).then_inc(mean_read, 1)
            dve.wait_ge(mean_read, 1)
            for c in range(CC):
                tt(dc[:, c, :], dc[:, c, :], t1, ALU.add).then_inc(centered, 1)
            dve.wait_ge(sd_ready, 1)
            link(nc.vector.reciprocal(cg, rg))
            for c in range(CC):
                tt(dc[:, c, :], dc[:, c, :], cg, ALU.mult).then_inc(scaled, 1)

            with dve.Fori(0, DC) as m:
                step.enter(m, 1)
                dve.wait_ge(sga_ready, m + 2)
                dve.wait_ge(ba_done, m + 2)
                tt(two(sga), halves[2], two(sga), ALU.mult).then_inc(a_gated, 1)
                dve.wait_ge(sgb_ready, m + 2)
                dve.wait_ge(bb_done, m + 2)
                link(tt(two(sgb), halves[3], two(sgb), ALU.mult))
                tt(merged[:, m, :], sga, sgb, ALU.add).then_inc(merged_ready, 1)
                step.leave(DC)

            with dve.Fori(0, 4) as i:
                for j in range(4):
                    dve.wait_ge(outX_done[j % 2], i * 2 + j // 2 + 2)
                    col = xt[:, :, bass.ds(i * 4 * P + j * P, P)]
                    tt(col, col, ps[:, 2 + j % 2, 0:TX].rearrange("p (t n) -> p t n", n=P),
                       ALU.add).then_inc(x1_ready[j % 2], 1)

            dve.wait_ge(rms_sqrt, 2)
            link(nc.vector.reciprocal(rstd, rstd))
            dve.wait_ge(gffn_in, 16)
            for t in range(NT):
                stt(out=xn[:, t, :], in0=xt[:, t, :], scalar=rstd[:, t:t + 1], in1=gffn,
                    op0=ALU.mult, op1=ALU.mult).then_inc(xn_ready, 1)
            nc.vector.memset(sc[:, 4 * HEADS:UNITS], 0.0).then_inc(sc_zero, 1)
            for k in range(1, DC, 2):
                dve.wait_ge(xT_done, DC + k + 1)
                nc.vector.tensor_copy(xnT[:, k, :], ps[:, k % 4, 0:T]).then_inc(xT_dve, 1)

            dve.wait_ge(sc_zero, 1)
            with dve.Fori(0, 4) as i:
                for j in range(4):
                    dve.wait_ge(s_done[j % 2], i * 2 + j // 2 + 2)
                    dve.wait_ge(s4_read[j % 2], i * 2 + j // 2 + 1)
                    own = sc[:, 4 * HEADS + j // 2, j % 2, :]
                    stt(out=own, in0=ps[:, 2 + j % 2, TP:TX], scalar=mask[:, bass.ds(i, 1)], in1=own,
                        op0=ALU.mult, op1=ALU.add).then_inc(s4_read[j % 2], 1)

            def top16(vals, spare, out_v, out_i):
                part(dve)
                link(nc.vector.max(out_v[:, 0:8], vals), alone=True)
                mark(nc.vector.max_index(out_i[:, 0:8], out_v[:, 0:8], vals))
                link(nc.vector.match_replace(spare, out_v[:, 0:8], vals, LOW), alone=True)
                link(nc.vector.max(out_v[:, 8:16], spare), alone=True)
                link(nc.vector.max_index(out_i[:, 8:16], out_v[:, 8:16], spare))

            def route(u, parity):
                dve.wait_ge(staged_scores, u + 1)
                for s in range(2):
                    top16(scur[:, s, :], swork[:, s, :], top[:, s, :], topi[:, s, :])
                mark(nc.vector.tensor_copy(topf, topi))
                link(tt(cand.rearrange("p (a b) -> p a b", a=TOPK),
                        top[:, 0, :].unsqueeze(2).to_broadcast([P, TOPK, TOPK]),
                        top[:, 1, :].unsqueeze(1).to_broadcast([P, TOPK, TOPK]), ALU.add))
                top16(cand, cwork, sv, si)
                ts_(nmax, sv[:, 0:1], -1.0, None, ALU.mult).then_inc(top_ready, 1)
                mark(ts_(ab[:, 0, :], si, 4, None, ALU.logical_shift_right))
                link(ts_(ab[:, 1, :], si, 15, None, ALU.bitwise_and))
                link(nc.vector.tensor_copy(abf, ab.rearrange("p s k -> p (s k)")))
                eq3 = eq.rearrange("p (a c) -> p a c", c=TOPK)
                eq4 = eq.rearrange("p (s a c) -> p s a c", s=2, c=TOPK)
                link(tt(eq3, abf.unsqueeze(2).to_broadcast([P, 2 * TOPK, TOPK]),
                        iota_s[:, :].unsqueeze(1).to_broadcast([P, 2 * TOPK, TOPK]), ALU.is_equal))
                link(tt(eq4, eq4, topf.unsqueeze(2).to_broadcast([P, 2, TOPK, TOPK]), ALU.mult))
                link(nc.vector.tensor_reduce(ei.rearrange("p s k -> p (s k)"), eq3, AX.X, ALU.add))
                if not isinstance(u, int) or u >= 2:
                    dve.wait_ge(idx_copied, u - 1)
                stt(out=idx_u[parity], in0=ei[:, 0, :], scalar=float(NK), in1=ei[:, 1, :],
                    op0=ALU.mult, op1=ALU.add).then_inc(idx_set, 1)
                dve.wait_ge(exp_ready, u + 1)
                link(nc.vector.reciprocal(ersum, esum))
                dve.wait_ge(idx_set, u + 1)
                ts_(gate[parity], ex16, ersum, None, ALU.mult).then_inc(routed, 1)

            def dot_unit(u, parity, route_next=True):
                for k in range(TOPK):
                    s = k % SLOTS
                    dve.wait_ge(u_landed[s], u * (16 * TOPK // SLOTS) + 16 * (k // SLOTS + 1))
                    stt(out=ubuf[s], in0=ubuf[s], scalar=1.0, in1=xn[:, u >> 3, :], op0=ALU.mult,
                        op1=ALU.mult, accum_out=dots[parity][:, k:k + 1]).then_inc(dot_done, 1)
                    if k == 3 and route_next:
                        route(u + 1, 1 - parity)

            def expert_weights(u, parity):
                dve.wait_ge(gelu_ready, u + 1)
                if not isinstance(u, int) or u >= 2:
                    dve.wait_ge(diag_ready, u * TOPK - TOPK + 1)
                dve.wait_ge(routed, u + 1)
                tt(wts[parity], gel, gate[parity], ALU.mult).then_inc(w_ready, 1)

            def add_unit(u, tile):
                dve.wait_ge(v_used, u * TOPK + TOPK)
                dve.wait_ge(acc_read, u + 1)
                tt(xt[:, tile, :], xt[:, tile, :], acc, ALU.add).then_inc(acc_read, 1)

            for j in range(2):
                dve.wait_ge(s4_read[j], HEADS + 1)
            route(0, 0)
            dot_unit(0, 0)
            expert_weights(0, 0)
            with dve.Fori(0, (UNITS - 2) // 2) as i:
                step.enter(i, 2 * 24)
                for n in (1, 2):
                    dot_unit(i * 2 + n, n % 2)
                    expert_weights(i * 2 + n, n % 2)
                    add_unit(i * 2 + (n - 1), (i * 2 + (n - 1)) >> 3)
                step.leave((UNITS - 2) // 2)
            dot_unit(UNITS - 1, 1, route_next=False)
            expert_weights(UNITS - 1, 1)
            add_unit(UNITS - 2, NT - 1)
            add_unit(UNITS - 1, NT - 1)

            dve.wait_ge(rms_sqrt, 3)
            link(nc.vector.reciprocal(rstd, rstd))
            dve.wait_ge(gfin_in, 16)
            for t in range(NT):
                stt(out=xt[:, t, :], in0=xt[:, t, :], scalar=rstd[:, t:t + 1], in1=gfin,
                    op0=ALU.mult, op1=ALU.mult).then_inc(y_ready, 1)

        @block.tensor
        def _(pe):
            for s in pe_counts:
                pe.sem_inc(s, 1)
            mm, tr = nc.tensor.matmul, nc.tensor.transpose
            pe.wait_ge(const_ready, 1)
            pe.wait_ge(keys_in, 32)
            for s in range(2):
                for h in range(HEADS):
                    last = tr(ps[:, s, h * P:(h + 1) * P], krows[:, s, h, :], ident)
                last.then_inc(stagedT, 1)
            pe.wait_ge(rows_in, 16 * 14)
            for c in range(CC):
                o = 512 * (c // 4) + R_N * (c % 4)
                last = tr(ps[:, 2, o:o + R_N], rows[0:R_N, c * P:(c + 1) * P], ident[0:R_N, 0:R_N])
            last.then_inc(stagedT, 1)
            for n, j in enumerate((3, 0)):
                if n:
                    pe.wait_ge(staged_read, 1)
                for c in range(4):
                    for a in range(2):
                        o = 512 * (c // 2) + 240 * (c % 2) + 120 * a
                        last = tr(ps[:, j, o:o + 120], cmrows[0:120, a, (4 * n + c) * P:(4 * n + c + 1) * P],
                                  ident[0:120, 0:120])
                last.then_inc(stagedT, 1)

            def tokens_to_channels(done):
                pe.wait_ge(xn_ready, (done + 1) * NT)
                for k in range(DC):
                    if k >= 4:
                        pe.wait_ge(xT_dve if k % 2 else xT_act, done * DC // 2 + (k - 4) // 2 + 1)
                    for t in range(NT - 1):
                        tr(ps[:, k % 4, t * P:(t + 1) * P], xn[:, t, k * P:(k + 1) * P], ident)
                    tr(ps[:, k % 4, TP:T], xn[0:TS, NT - 1, k * P:(k + 1) * P],
                       ident[0:TS, 0:TS]).then_inc(xT_done, 1)
                pe.wait_ge(xT_act, (done + 1) * DC // 2)
                pe.wait_ge(xT_dve, (done + 1) * DC // 2)

            pe.wait_ge(staged_read, 5)
            tokens_to_channels(0)

            def product(j, slot, rhs, chunks):
                for k in range(chunks):
                    for a in range(2):
                        last = mm(halves[j][:, a, :], wslot[slot][:, k, :], rhs[:, k, a * TH:(a + 1) * TH],
                                  start=(k == 0), stop=(k == chunks - 1))
                return last

            xc_s = xcv[:, TP + RW - 1:TP + RW - 1 + NB * RPAD].rearrange("p (b j) -> p b j", j=RPAD)[:, :, 0:NS]
            with pe.Fori(0, CC) as c:
                pe.wait_ge(w_landed[0], c * 16 + 16)
                pe.wait_ge(rg_ready, c + 1)
                product(0, 0, xnT, DC).then_inc(xr_done, 1)
                pe.wait_ge(w_landed[1], c * 16 + 16)
                pe.wait_ge(ig_ready, c + 1)
                product(1, 1, xnT, DC).then_inc(yr_done, 1)
                pe.wait_ge(w_landed[2], c * 16 + 16)
                pe.wait_ge(glu_ready, c + 1)
                product(2, 2, xnT, DC).then_inc(ca_done, 1)
                pe.wait_ge(gw_landed, c * 32 + 32)
                pe.wait_ge(xcv_ready, c + 2)
                for s, (read, done) in enumerate(((xr_padded, rgate_done), (yg_ready, igate_done))):
                    pe.wait_ge(read, c + 1)
                    mm(ps[:, s, 0:TP], gw[:, s, :], xcv[:, 0:TP], start=True, stop=True)
                    mm(ps[:, s, TP:T].rearrange("p (b s) -> p b s", s=NS), gw[:, s, :], xc_s,
                       start=True, stop=True).then_inc(done, 1)
                pe.wait_ge(w_landed[3], c * 16 + 16)
                pe.wait_ge(cg_ready, c + 1)
                product(3, 3, xnT, DC).then_inc(cb_done, 1)

            pe.wait_ge(dc_ready, CC)
            pe.wait_ge(rg_ready, CC + 1)
            for c in range(CC):
                for a in range(2):
                    last = mm(halves[0][:, a, :], ones[:, :], dc[:, c, a * TH:(a + 1) * TH],
                              start=(c == 0), stop=(c == CC - 1))
            last.then_inc(mean_done, 1)
            pe.wait_ge(glu_ready, CC + 1)
            for c in range(CC):
                last = tr(ps[0:E_N, 2, c * P:(c + 1) * P], ex[:, c, :], ident)
            last.then_inc(exT_done, 1)
            pe.wait_ge(ig_ready, CC + 1)
            sqb = (th, t2)
            for c in range(CC):
                pe.wait_ge(sq_ready, c + 1)
                for a in range(2):
                    last = mm(halves[1][:, a, :], ones[:, :], sqb[c % 2][:, a * TH:(a + 1) * TH],
                              start=(c == 0), stop=(c == CC - 1))
                last.then_inc(sq_used, 1)

            pe.wait_ge(mean_read, 1)
            pe.wait_ge(sd_ready, 1)
            pe.wait_ge(exT_read, 1)
            pe.wait_ge(cg_ready, CC + 1)
            with pe.Fori(0, DC) as m:
                pe.wait_ge(w_landed[0], m * 16 + (CC + 1) * 16)
                pe.wait_ge(sga_ready, m + 1)
                product(0, 0, xnT, DC).then_inc(ga_done, 1)
                pe.wait_ge(w_landed[1], m * 16 + (CC + 1) * 16)
                pe.wait_ge(sgb_ready, m + 1)
                product(1, 1, xnT, DC).then_inc(gb_done, 1)
                pe.wait_ge(w_landed[2], m * 16 + (CC + 1) * 16)
                pe.wait_ge(a_gated, m + 1)
                product(2, 2, ha, CC).then_inc(ba_done, 1)
                pe.wait_ge(w_landed[3], m * 16 + (CC + 1) * 16)
                pe.wait_ge(merged_ready, m + 1)
                pe.wait_ge(silu_ready, CC)
                product(3, 3, dc, CC).then_inc(bb_done, 1)

            def blocks(i, rhs, landed, done, ready, after):
                for j in range(4):
                    pe.wait_ge(w_landed[j], i * 16 + (landed + 1) * 16)
                    pe.wait_ge(ready[j % 2], i * 2 + j // 2 + 1)
                    product(j % 2, j, rhs, DC).then_inc(done, 1)
                    if j:
                        after(i, j - 1)
                after(i, 3)

            def back_to_tokens(i, j):
                pe.wait_ge(outT_ready[j % 2], i * 2 + j // 2 + 2)
                pe.wait_ge(x1_ready[j % 2], i * 2 + j // 2 + 1)
                for t in range(NT):
                    last = tr(ps[:, 2 + j % 2, t * P:(t + 1) * P], blockT[j % 2][:, t * P:(t + 1) * P], ident)
                last.then_inc(outX_done[j % 2], 1)

            def score(i, j):
                pe.wait_ge(qT_ready[j % 2], i * 2 + j // 2 + 2)
                pe.wait_ge(s_read[j % 2], i * 2 + j // 2 + 1)
                pe.wait_ge(s4_read[j % 2], i * 2 + j // 2 + 1)
                for t in range(NT):
                    last = mm(ps[:, 2 + j % 2, t * P:(t + 1) * P], blockT[j % 2][:, t * P:(t + 1) * P],
                              keysT[:, j % 2, i * 2 + j // 2, :], start=True, stop=True)
                last.then_inc(s_done[j % 2], 1)

            pe.wait_ge(merged_ready, DC + 1)
            with pe.Fori(0, 4) as i:
                blocks(i, merged, CC + DC, out_done, outT_ready, back_to_tokens)
            tokens_to_channels(1)
            with pe.Fori(0, 4) as i:
                blocks(i, xnT, CC + DC + 4, q_done, qT_ready, score)

            for j in range(2):
                pe.wait_ge(s4_read[j], HEADS + 1)
                pe.wait_ge(qT_ready[j], HEADS + 1)
            with pe.Fori(0, UNITS // 2) as i:
                for n in range(2):
                    u = i * 2 + n
                    pe.wait_ge(acc_read, u + 1)
                    for k in range(TOPK):
                        s = k % SLOTS
                        pe.wait_ge(diag_ready, u * TOPK + (k + 2))
                        pe.wait_ge(v_landed[s], u * (16 * TOPK // SLOTS) + 16 * (k // SLOTS + 1))
                        for b in range(4):
                            last = mm(acc[:, b * 512:(b + 1) * 512], diag[:, k, :],
                                      vbuf[s][:, b * 512:(b + 1) * 512], start=(k == 0), stop=(k == TOPK - 1))
                        last.then_inc(v_used, 1)


_INS = ['x_prompt', 'x_sample', 'state_rnn_conv', 'state_rnn_h', 'state_cm_conv', 'g_mix', 'w_in',
        'w_rconv', 'b_rconv', 'w_r', 'b_r', 'w_i', 'b_i', 'lam', 'w_a', 'w_cconv', 'b_cconv', 'ln_g',
        'ln_b', 'w_b', 'w_out', 'g_ffn', 'w_q', 'keys1', 'keys2', 'u_tab', 'v_tab', 'g_final']
_OUTS = [(1, TP, D), (NB, NS, D), (1, 1, RW - 1, CH), (1, 1, CH), (1, 1, CW - 1, CH),
         (1, NB, RW - 1, CH), (1, NB, CH), (1, NB, CW - 1, CH)]


def kernel(**inputs):
    import numpy as _np
    import concourse.bacc as _bacc
    from concourse.bass_utils import run_bass_kernel_spmd as _run

    nc = _bacc.Bacc("TRN2", target_bir_lowering=False, num_devices=1)
    arrays, args = {}, []
    for name in _INS:
        a = _np.ascontiguousarray(inputs[name])
        arrays[f"in_{name}_dram"] = a
        args.append(nc.dram_tensor(f"in_{name}_dram", a.shape, mybir.dt.from_np(a.dtype), kind="ExternalInput").ap())
    for i, shape in enumerate(_OUTS):
        args.append(nc.dram_tensor(f"out_{i}_dram", shape, F32, kind="ExternalOutput").ap())
    hybrid_step(nc, *args)
    r = _run(nc, [arrays], core_ids=[0])
    return tuple(r.results[0][f"out_{i}_dram"] for i in range(len(_OUTS)))
```

```python
import concourse.bass as bass
from concourse import mybir
from contextlib import ExitStack

F32 = mybir.dt.float32
F32R = mybir.dt.float32r
I32 = mybir.dt.int32
U32 = mybir.dt.uint32
ALU = mybir.AluOpType
ACT = mybir.ActivationFunctionType
AX = mybir.AxisListType

P = 128
D = 2048
DC = D // P
CH = 1024
CC = CH // P
TP = 512
NB, NS = 8, 4
TS = NB * NS
T = TP + TS
TH = T // 2
TX = TP + P
NT = TX // P
RW, CW = 4, 31
RPAD = RW - 1 + NS
CPAD = CW - 1 + NS
RFLAT = RW - 1 + TP + NB * RPAD
CFLAT = CW - 1 + TP + NB * CPAD
SCAN = TP + NB * (NS + 1)
NK = 128
HEADS = 8
TOPK = 16
UNITS = 4 * HEADS + 2
SLOTS = 4
EPS = 1e-6
LRU_C = 8.0
LOW = -3.0e38
PAIR = ((0, 1), (2, 3))
USES = (0, 2 * CC, 2 * CC + 3 * DC // 2, 2 * CC + 3 * DC // 2 + 8)
SPLITS = (0, 2 * CC, 2 * CC + DC, 2 * CC + DC + DC // 2)
PER_ROUTE = 26
PER_CHUNK = 20 + CW + 1
ARENA_AT = 16512
ARENA = 53072
KP = 8
PIECE = KP * P
LEAD = HEADS
CATCH = 6
SPARE = LEAD + CATCH - 2 * CATCH

R_WR, R_BR, R_BRG, R_BIG, R_LAM = 0, 4, 5, 6, 7
R_WC, R_BC, R_LNG, R_LNB, R_GM = 8, 39, 40, 41, 42
R_SRC, R_SH, R_N = 44, 68, 76
E_RCP, E_CCP, E_HP, E_RCS, E_CCS, E_HS, E_N = 0, 3, 33, 34, 58, 90, 98


class Steps:

    def __init__(self, eng, sem):
        self.eng, self.sem, self.base, self.n = eng, sem, 0, 0

    def mark(self, ins):
        ins.then_inc(self.sem, 1)
        self.n += 1

    def link(self, ins, alone=False):
        self.mark(ins)
        self.eng.wait_ge(self.sem, self.base + self.n)
        if alone:
            part(self.eng)

    def enter(self, i, per):
        self.start, self.per = self.base + self.n, per
        self.base, self.n = i * per + self.start, 0

    def leave(self, trips):
        assert self.n == self.per, (self.n, self.per)
        self.base, self.n = self.start + trips * self.per, 0


def part(eng):
    eng.nop(nofuse=True)


def hybrid_step(nc, x_prompt, x_sample, state_rnn_conv, state_rnn_h, state_cm_conv, g_mix, w_in,
                w_rconv, b_rconv, w_r, b_r, w_i, b_i, lam, w_a, w_cconv, b_cconv, ln_g, ln_b, w_b,
                w_out, g_ffn, w_q, keys1, keys2, u_tab, v_tab, g_final,
                y_prompt, y_sample, rc_p, h_p, cc_p, rc_s, h_s, cc_s):
    w_in_v = w_in.rearrange("l (k p) n -> p (l k) n", p=P)
    w_a_v = w_a.rearrange("l (k p) n -> p (l k) n", p=P)
    w_b_v = w_b.rearrange("l (k p) n -> p (l k) n", p=P)
    w_out_v = w_out.rearrange("l (k p) n -> p (l k) n", p=P)
    w_q_v = w_q.rearrange("l (k p) n -> p (l k) n", p=P)
    w_r_v = w_r.rearrange("l h i j -> i (l h) j")
    w_i_v = w_i.rearrange("l h i j -> i (l h) j")
    u_rows = u_tab.rearrange("l e d -> (l e) d")
    v_rows = v_tab.rearrange("l e d -> (l e) d")
    xs_rows = x_sample.rearrange("b s d -> (b s) d")

    with ExitStack() as ctx:
        def sb(name, n, dt=F32):
            return ctx.enter_context(nc.sbuf_tensor(name, [P, n], dt))

        def sem(name):
            return ctx.enter_context(nc.semaphore(name))

        sb("arena", ARENA)
        regions = []

        def region(at, n, dt=F32):
            regions.append(nc.alloc_sbuf_tensor_at(f"region{len(regions)}", [P, n], dt, offset=ARENA_AT + 4 * at))
            return regions[-1][:, :]

        o_w = 2 * DC * T
        o_2 = o_w + 8 * PIECE
        o_3 = o_2 + NT * D
        o_k = o_3 + NT * D
        o_f = o_k + 2048
        o_g = o_f + 2 * TX
        o_m = o_g + 1216
        xh = region(0, DC * T, F32R).rearrange("p (k t) -> p k t", t=T)
        xl = region(DC * T, DC * T, F32R).rearrange("p (k t) -> p k t", t=T)
        xh_f = xh.bitcast(F32)
        wlo_t = region(o_w, 4 * PIECE, F32R)
        whi_t = region(o_w + 4 * PIECE, 4 * PIECE, F32R)
        wlo = [wlo_t[:, s * PIECE:(s + 1) * PIECE] for s in range(4)]
        whi = [whi_t[:, s * PIECE:(s + 1) * PIECE] for s in range(4)]
        wraw = [region(o_w + s * PIECE, PIECE) for s in range(4)]
        whi_f = [whi[s].bitcast(F32) for s in range(4)]
        sc = region(0, UNITS * 2 * NK).rearrange("p (u s k) -> p u s k", s=2, k=NK)
        junk = region(0, D)
        xnT = region(DC * T, DC * T).rearrange("p (k t) -> p k t", t=T)
        xf = region(DC * T, NT * D).rearrange("p (t d) -> p t d", d=D)
        vbuf = [region(DC * T + NT * D + s * D if s < SLOTS - 1 else o_3 + SLOTS * D, D) for s in range(SLOTS)]
        assert DC * T + NT * D + (SLOTS - 1) * D <= o_2
        reg_d = region(o_2, NT * D)
        xn = reg_d.rearrange("p (t d) -> p t d", d=D)
        merged = reg_d[:, 0:DC * T].rearrange("p (m t) -> p m t", t=T)
        gffn, gfin = xn[:, NT - 1, :], xn[:, 0, :]
        reg_c = region(o_3, NT * D)
        xt = reg_c.rearrange("p (t d) -> p t d", d=D)
        ha = reg_c[:, 0:CC * T].rearrange("p (c t) -> p c t", t=T)
        dc = reg_c[:, CC * T:2 * CC * T].rearrange("p (c t) -> p c t", t=T)
        ex = reg_c[:, 2 * CC * T:2 * CC * T + CC * E_N].rearrange("p (c e) -> p c e", e=E_N)
        ubuf = [region(o_3 + s * D, D) for s in range(SLOTS)]
        reg_k = region(o_k, 2048)
        reg_f = region(o_f, 2 * TX)
        reg_g = region(o_g, 1216)
        keysT = reg_k.rearrange("p (s h k) -> p s h k", s=2, h=HEADS)
        diag = reg_k.rearrange("p (k m) -> p k m", m=P)

        rows = reg_d[:, 0:CH]
        cmrows = reg_d[:, CH:3 * CH].rearrange("p (a n) -> p a n", a=2)
        krows = reg_d[:, 3 * CH:5 * CH].rearrange("p (s h d) -> p s h d", s=2, h=HEADS)

        at = [0]

        def cut(n):
            at[0] += n
            return reg_d[:, at[0] - n:at[0]]

        yg, rg, ig, th, t1, t2, cg = (cut(T) for _ in range(7))
        xcv, bb, hh, acc31 = cut(576), cut(SCAN), cut(SCAN), cut(816)
        assert at[0] >= 5 * CH
        xrpad, glupad, aa = cut(576), cut(816), cut(SCAN)
        cmT = cut(CC * NB * (CW - 1)).rearrange("p (c e) -> p c e", c=CC)
        assert at[0] <= NT * D
        sga, sgb = reg_f[:, 0:T], reg_f[:, T:2 * T]
        blockT = [reg_f[:, j * TX:(j + 1) * TX] for j in range(2)]

        atm = [0]
        reg_m = region(o_m, ARENA - o_m)

        def cutm(n):
            atm[0] += n
            return reg_m[:, atm[0] - n:atm[0]]

        w_all = cutm(UNITS * TOPK)
        idx_all = cutm(UNITS * TOPK).bitcast(I32)
        sel_t, ones, par_t, gw_t, small, iota_s = cutm(2 * P), cutm(P), cutm(CC * R_N), cutm(2 * P), cutm(96), cutm(16)
        assert atm[0] <= ARENA - o_m
        rows_out = reg_g[:, 0:CH]
        sel = sel_t.rearrange("p (s m) -> p s m", s=2)
        ident = sel[:, 0, :]
        par = par_t.rearrange("p (c r) -> p c r", r=R_N)
        gw = gw_t.rearrange("p (s j) -> p s j", s=2)
        cneg, cpos = small[:, 0:8], small[:, 8:16]
        sp_a, sp_b, sp_c, sp_d = (small[:, 16 + 8 * j:24 + 8 * j] for j in range(4))
        ssq, rstd, eps = small[:, 48:53], small[:, 56:61], small[:, 64:65]
        mask = small[:, 68:72]

        at2 = [0]

        def cutf(n, dt=None):
            at2[0] += n
            v = reg_g[:, at2[0] - n:at2[0]]
            return v if dt is None else v.bitcast(dt)

        eq = cutf(512)
        scur = eq[:, 0:256].rearrange("p (s k) -> p s k", s=2)
        swork, cwork = eq[:, 256:512].rearrange("p (s k) -> p s k", s=2), eq[:, 256:512]
        cand = cutf(256)
        top = cutf(32).rearrange("p (s k) -> p s k", s=2)
        topi = cutf(32, U32).rearrange("p (s k) -> p s k", s=2)
        topf = cutf(32).rearrange("p (s k) -> p s k", s=2)
        sv, si = cutf(16), cutf(16, U32)
        ab = cutf(32, U32).rearrange("p (s k) -> p s k", s=2)
        abf, ei = cutf(32), cutf(32).rearrange("p (s k) -> p s k", s=2)
        idx_u = [cutf(16, I32) for _ in range(2)]
        idx_v = [cutf(16, I32) for _ in range(2)]
        dots = [cutf(16) for _ in range(2)]
        gate = [cutf(16) for _ in range(2)]
        gel, ex16, nmax, esum, ersum = cutf(16), cutf(16), cutf(1), cutf(1), cutf(1)
        assert at2[0] <= 1216

        ps = ctx.enter_context(nc.psum_tensor("ps", [P, 4, 1024], F32))
        halves = [ps[:, j, :].rearrange("p (a n) -> p a n", a=2)[:, :, 0:TH] for j in range(4)]
        acc = [ps[:, 2 * j:2 * j + 2, :].rearrange("p a n -> p (a n)") for j in range(2)]

        const_ready = sem("const_ready")
        rows_in, cm_in, keys_in = sem("rows_in"), sem("cm_in"), sem("keys_in")
        x_in = [sem(f"x_in{t}") for t in range(NT)]
        ssq_ready, rms_sqrt, xn_ready = sem("ssq_ready"), sem("rms_sqrt"), sem("xn_ready")
        stagedT, staged_read = sem("stagedT"), sem("staged_read")
        xT_done, xT_act, xT_dve = sem("xT_done"), sem("xT_act"), sem("xT_dve")
        exp_lam, lam_abs, lru_ready = sem("exp_lam"), sem("lam_abs"), sem("lru_ready")
        w_landed = [sem(f"w_landed{s}") for s in range(4)]
        hi_ready = [sem(f"hi_ready{s}") for s in range(4)]
        lo_ready = [sem(f"lo_ready{s}") for s in range(4)]
        half_used = [sem(f"half_used{p}") for p in range(2)]
        mhi_ready, mlo_ready, x_again, x1_out, x1_back = (sem(n) for n in (
            "mhi_ready", "mlo_ready", "x_again", "x1_out", "x1_back"))
        gw_landed = sem("gw_landed")
        xr_done, yr_done, ca_done, cb_done = sem("xr_done"), sem("yr_done"), sem("ca_done"), sem("cb_done")
        rgate_done, igate_done = sem("rgate_done"), sem("igate_done")
        xr_padded, yg_ready, xcv_ready = sem("xr_padded"), sem("yg_ready"), sem("xcv_ready")
        rg_ready, ig_ready, decay_ready = sem("rg_ready"), sem("ig_ready"), sem("decay_ready")
        beta2_ready, beta_ready, ha_ready = sem("beta2_ready"), sem("beta_ready"), sem("ha_ready")
        cg_ready, glu_ready, dc_ready = sem("cg_ready"), sem("glu_ready"), sem("dc_ready")
        mean_done, mean_read, centered = sem("mean_done"), sem("mean_read"), sem("centered")
        sq_ready, sq_used, sd_ready = sem("sq_ready"), sem("sq_used"), sem("sd_ready")
        scaled, silu_ready = sem("scaled"), sem("silu_ready")
        exT_done, exT_read = sem("exT_done"), sem("exT_read")
        ga_done, gb_done, ba_done, bb_done = sem("ga_done"), sem("gb_done"), sem("ba_done"), sem("bb_done")
        sga_ready, sgb_ready = sem("sga_ready"), sem("sgb_ready")
        a_gated, merged_ready = sem("a_gated"), sem("merged_ready")
        out_done = sem("out_done")
        outT_ready = [sem(f"outT_ready{j}") for j in range(2)]
        outX_done = [sem(f"outX_done{j}") for j in range(2)]
        x1_ready = [sem(f"x1_ready{j}") for j in range(2)]
        gffn_in, gfin_in = sem("gffn_in"), sem("gfin_in")
        q_done = sem("q_done")
        qT_ready = [sem(f"qT_ready{j}") for j in range(2)]
        s_done = [sem(f"s_done{j}") for j in range(2)]
        s_read = [sem(f"s_read{j}") for j in range(2)]
        s4_read = [sem(f"s4_read{j}") for j in range(2)]
        sc_zero = sem("sc_zero")
        u_landed = [sem(f"u_landed{s}") for s in range(SLOTS)]
        v_landed = [sem(f"v_landed{s}") for s in range(SLOTS)]
        staged_scores, top_ready, exp_ready = sem("staged_scores"), sem("top_ready"), sem("exp_ready")
        routed, idx_copied = sem("routed"), sem("idx_copied")
        dot_done, gelu_ready, w_ready = sem("dot_done"), sem("gelu_ready"), sem("w_ready")
        diag_ready, v_used, acc_read = sem("diag_ready"), sem("v_used"), sem("acc_read")
        y_ready = sem("y_ready")
        out_p, out_a = sem("out_p"), sem("out_a")
        dve_step, pool_step = sem("dve_step"), sem("pool_step")

        pe_counts = [ca_done, cb_done, xr_done, yr_done, igate_done, ga_done, gb_done, ba_done, bb_done,
                     *outX_done, *s_done, *half_used]
        act_counts = [rg_ready, ig_ready, cg_ready, sga_ready, sgb_ready, *outT_ready, *qT_ready, *s_read]
        dve_counts = [glu_ready, ha_ready, xcv_ready, merged_ready, a_gated, w_ready, *x1_ready, *s4_read]

        x1_d = nc.dram_tensor("x1_kept", (P, NT * D), F32, kind="Internal").ap()

        block = ctx.enter_context(nc.Block())

        @block.sync
        def _(sp):
            for t in range(NT - 1):
                sp.dma_start(xt[:, t, :], x_prompt[0, t * P:(t + 1) * P, :]).then_inc(x_in[t], 16)
            for g in range(4):
                sp.dma_start(xt[g * TS:(g + 1) * TS, NT - 1, :], xs_rows).then_inc(x_in[NT - 1], 16)
            for r, src in [(R_WR, w_rconv[0]), (R_BR, b_rconv), (R_BRG, b_r), (R_BIG, b_i), (R_LAM, lam),
                           (R_WC, w_cconv[0]), (R_BC, b_cconv), (R_LNG, ln_g), (R_LNB, ln_b),
                           (R_GM, g_mix.rearrange("l (a n) -> (l a) n", n=CH)),
                           (R_SRC, state_rnn_conv.rearrange("l b j n -> (l b j) n")), (R_SH, state_rnn_h[0])]:
                sp.dma_start(rows[r:r + src.shape[0], :], src).then_inc(rows_in, 16)

            def piece(s, w, half, col, free):
                sp.wait_ge(*free)
                part(sp)
                cols = bass.ds(col, P) if not isinstance(col, int) else slice(col, col + P)
                sp.dma_start(wraw[s].rearrange("p (k n) -> p k n", n=P),
                             w[:, half * KP:(half + 1) * KP, cols]).then_inc(w_landed[s], 16)

            def block_of(pair, w, col, free0, free1):
                piece(PAIR[pair][0], w, 0, col, free0)
                piece(PAIR[pair][1], w, 1, col, free1)

            with sp.Fori(0, CC) as c:
                block_of(0, w_in_v, c * P, (half_used[0], c * 2 + 1), (ca_done, c + 1))
                block_of(1, w_in_v, c * P + CH, (half_used[1], c * 2 + 1), (cb_done, c + 1))
                sp.wait_ge(igate_done, c + 1)
                sp.dma_start(gw[:, 0, :], w_r_v[:, c, :]).then_inc(gw_landed, 16)
                sp.dma_start(gw[:, 1, :], w_i_v[:, c, :]).then_inc(gw_landed, 16)
                block_of(0, w_in_v, c * P + 2 * CH, (half_used[0], c * 2 + 2), (xr_done, c + 2))
                block_of(1, w_in_v, c * P + 3 * CH, (half_used[1], c * 2 + 2), (yr_done, c + 2))
            sp.wait_ge(ca_done, CC + 1)
            sp.wait_ge(cb_done, CC + 1)
            with sp.Fori(0, DC // 2) as i:
                m, q = i * 2, i * 2 + SPLITS[1]
                block_of(0, w_in_v, i * 2 * P + 4 * CH, (half_used[0], q + 1), (gb_done, m + 1))
                block_of(1, w_in_v, i * 2 * P + (4 * CH + D), (ba_done, m + 1), (bb_done, m + 1))
                piece(0, w_a_v, 0, i * 2 * P, (half_used[0], q + 2))
                piece(1, w_b_v, 0, i * 2 * P, (ga_done, m + 2))
                block_of(1, w_in_v, i * 2 * P + (4 * CH + P), (half_used[1], q + 2), (gb_done, m + 2))
                block_of(0, w_in_v, i * 2 * P + (4 * CH + D + P), (ba_done, m + 2), (bb_done, m + 2))
                piece(2, w_a_v, 0, i * 2 * P + P, (half_used[1], q + 3))
                piece(3, w_b_v, 0, i * 2 * P + P, (ga_done, m + 3))
            for last_product in (gb_done, ba_done, bb_done):
                sp.wait_ge(last_product, DC + 1)
            with sp.Fori(0, 4) as i:
                for j in range(4):
                    block_of(j % 2, w_out_v, i * 4 * P + j * P,
                             (half_used[j % 2], i * 2 + (SPLITS[2] + j // 2 + 1)), (out_done, i * 4 + (j + 1)))
            sp.wait_ge(mlo_ready, DC)
            sp.dma_start(gffn, g_ffn.partition_broadcast(P)).then_inc(gffn_in, 16)
            sp.wait_ge(out_done, DC + 2)
            with sp.Fori(0, HEADS) as i:
                for j in range(2):
                    block_of(j, w_q_v, i * 2 * P + j * P,
                             (half_used[j], i + (SPLITS[3] + 1)), (q_done, i * 2 + (j + 1)))
            sp.wait_ge(q_done, DC + 2)
            sp.wait_ge(x1_out, 16)
            sp.dma_start(xf.rearrange("p t d -> p (t d)"), x1_d).then_inc(x1_back, 16)
            sp.wait_ge(dot_done, TOPK * HEADS + SLOTS)
            sp.dma_start(gfin, g_final.partition_broadcast(P)).then_inc(gfin_in, 16)
            for t in range(NT - 1):
                sp.wait_ge(y_ready, t + 1)
                sp.dma_start(y_prompt[0, t * P:(t + 1) * P, :], xf[:, t, :]).then_inc(out_p, 16)
            sp.wait_ge(y_ready, NT)
            sp.dma_start(y_sample.rearrange("b s d -> (b s) d"), xf[0:TS, NT - 1, :]).then_inc(out_p, 16)
            sp.wait_ge(out_p, 16 * NT)

        @block.gpsimd
        def _(pool):
            step = Steps(pool, pool_step)
            step.link(nc.gpsimd.memset(ones, 1.0))
            step.link(nc.gpsimd.memset(small[:, 64:65], EPS))
            step.link(nc.gpsimd.memset(mask, 0.0))
            step.link(nc.gpsimd.memset(sel_t, 0.0))
            step.link(nc.gpsimd.affine_select(out=ident, in_=ident, compare_op=ALU.not_equal, fill=1.0,
                                              base=0, pattern=[[-1, P]], channel_multiplier=1))
            for g in range(4):
                q = slice(g * TS, (g + 1) * TS)
                step.link(nc.gpsimd.memset(mask[q, g:g + 1], 1.0))
                step.link(nc.gpsimd.tensor_copy(sel[q, 1, 0:TS], ident[q, q]))
            step.link(nc.gpsimd.iota(iota_s, pattern=[[1, TOPK]], base=0, channel_multiplier=0,
                                     allow_small_or_imprecise_dtypes=True))
            step.link(nc.gpsimd.memset(xrpad[:, 0:RW - 1], 0.0))
            step.link(nc.gpsimd.memset(glupad[:, 0:CW - 1], 0.0))
            nc.gpsimd.memset(aa, 0.0).then_inc(const_ready, 1)
            cm = state_cm_conv.rearrange("l (a b) j n -> a (l b j) n", a=2)
            for a in range(2):
                pool.dma_start(cmrows[0:NB * (CW - 1) // 2, a, :], cm[a]).then_inc(cm_in, 16)
            pool.dma_start(krows[:, 0], keys1.rearrange("l h k d -> k (l h) d")).then_inc(keys_in, 16)
            pool.dma_start(krows[:, 1], keys2.rearrange("l h k d -> k (l h) d")).then_inc(keys_in, 16)

            def gather(rows_ap, slot, landed, idx, k):
                part(pool)
                pool.indirect_dma_start(out=slot, out_offset=None, in_=rows_ap,
                                        in_offset=bass.IndirectOffsetOnAxis(ap=idx[:, k:k + 1], axis=0)
                                        ).then_inc(landed, 16)

            def low(slots, n):
                for s in slots:
                    pool.wait_ge(hi_ready[s], n + 1)
                    nc.gpsimd.tensor_tensor(wlo[s], wraw[s], whi_f[s], ALU.subtract).then_inc(lo_ready[s], 1)

            with pool.Fori(0, CC) as c:
                for pair, n in ((0, 0), (1, 0), (0, 1), (1, 1)):
                    low(PAIR[pair], c * 2 + n)
            with pool.Fori(0, DC // 2) as i:
                for pair, n in ((0, 0), (1, 0), (1, 1), (0, 1)):
                    low(PAIR[pair], i * 2 + (SPLITS[1] + n))
            for j in range(2):
                low(PAIR[j], SPLITS[2])
            pool.wait_ge(bb_done, DC + 1)
            for t in range(NT - 1):
                pool.dma_start(xt[:, t, :], x_prompt[0, t * P:(t + 1) * P, :]).then_inc(x_again, 16)
            for g in range(4):
                pool.dma_start(xt[g * TS:(g + 1) * TS, NT - 1, :], xs_rows).then_inc(x_again, 16)
            for j in range(2):
                low(PAIR[j], SPLITS[2] + 1)
            with pool.Fori(1, 4) as i:
                for j in range(4):
                    low(PAIR[j % 2], i * 2 + (SPLITS[2] + j // 2))

            def u_row(u, parity, k):
                s = k % SLOTS
                pool.wait_ge(dot_done, u * TOPK + (k + 1))
                gather(u_rows, ubuf[s], u_landed[s], idx_u[parity], k)

            def v_row(v, parity, k):
                s = k % SLOTS
                pool.wait_ge(v_used, v * TOPK + (k - SLOTS + 1 + TOPK))
                gather(v_rows, vbuf[s], v_landed[s], idx_v[parity], k)

            def v_indices(v, parity):
                nc.gpsimd.tensor_copy(idx_v[parity], idx_all[:, bass.ds(v * TOPK, TOPK)]).then_inc(idx_copied, 1)
                pool.wait_ge(idx_copied, v + 1)

            pool.wait_ge(x1_out, 16)
            with pool.Fori(0, LEAD // 2) as i:
                for n in range(2):
                    pool.wait_ge(routed, i * 2 + (n + 1))
                    for k in range(TOPK):
                        u_row(i * 2 + n, n, k)
            pool.wait_ge(q_done, DC + 2)
            with pool.Fori(0, CATCH // 2) as i:
                for n in range(2):
                    u, v = i * 2 + (LEAD + n), i * 4 + 2 * n
                    pool.wait_ge(routed, u + 1)
                    v_indices(v, 0)
                    for k in range(TOPK):
                        u_row(u, n, k)
                        if k == TOPK // 2:
                            v_indices(v + 1, 1)
                        for a in (2 * k, 2 * k + 1):
                            v_row(v + a // TOPK, a // TOPK, a % TOPK)
            with pool.Fori(0, (UNITS - LEAD - CATCH) // 2) as i:
                for n in range(2):
                    u = i * 2 + (LEAD + CATCH + n)
                    pool.wait_ge(routed, u + 1)
                    v_indices(u - SPARE, n)
                    for k in range(TOPK):
                        u_row(u, n, k)
                        v_row(u - SPARE, n, k)
            for v in range(UNITS - SPARE, UNITS):
                v_indices(v, v % 2)
                for k in range(TOPK):
                    v_row(v, v % 2, k)

        @block.scalar
        def _(act):
            for s in act_counts:
                act.sem_inc(s, 1)

            def high(slots, use):
                for s in slots:
                    act.wait_ge(w_landed[s], use * 16 + 16)
                    nc.scalar.activation(whi[s], wraw[s], ACT.Copy).then_inc(hi_ready[s], 1)

            def sum_squares(t, x, n):
                act.wait_ge(ssq_ready, n * NT + t)
                nc.scalar.activation(junk, x[:, t, :], ACT.Square, accum_out=ssq[:, t:t + 1]).then_inc(ssq_ready, 1)

            def root(n, tiles=slice(0, NT)):
                act.wait_ge(ssq_ready, (n - 1) * NT + tiles.stop)
                nc.scalar.activation(rstd[:, tiles], ssq[:, tiles], ACT.Sqrt, bias=eps, scale=1.0 / D).then_inc(rms_sqrt, 1)

            act.wait_ge(const_ready, 1)
            for t in range(NT):
                act.wait_ge(x_in[t], 64 if t == NT - 1 else 16)
                sum_squares(t, xt, 0)
            root(1)
            act.wait_ge(stagedT, 1)
            for b in range(2):
                last = nc.scalar.activation(par[:, 4 * b:4 * b + 4, :],
                                            ps[:, 2, 512 * b:512 * b + 4 * R_N].rearrange("p (c r) -> p c r", r=R_N),
                                            ACT.Copy)
            last.then_inc(staged_read, 1)
            act.wait_ge(staged_read, 1)
            for k in range(DC):
                act.wait_ge(xT_done, k + 1)
                nc.scalar.activation(xh[:, k, :], ps[:, k % 4, 0:T], ACT.Copy,
                                     scale=par[:, k % CC, R_GM + k // CC:R_GM + k // CC + 1]).then_inc(xT_act, 1)
                if k == 1:
                    high(PAIR[0], 0)
            for n in range(2):
                act.wait_ge(stagedT, 2 + n)
                for b in range(2):
                    c = 4 * n + 2 * b
                    last = nc.scalar.activation(cmT[:, c:c + 2, :],
                                                ps[:, n, 512 * b:512 * b + 480].rearrange("p (c r) -> p c r", r=240),
                                                ACT.Copy)
                last.then_inc(staged_read, 1)
            for s in range(2):
                act.wait_ge(stagedT, 4 + s)
                nc.scalar.activation(keysT[:, s].rearrange("p h k -> p (h k)"), ps[:, 2 + s, :], ACT.Copy).then_inc(staged_read, 1)
            act.wait_ge(lam_abs, 1)
            nc.scalar.activation(sp_b, sp_a, ACT.Exp, scale=-1.0).then_inc(exp_lam, 1)

            act.wait_ge(lru_ready, 1)
            xr_s = xrpad[:, RW - 1 + TP:RFLAT].rearrange("p (b j) -> p b j", j=RPAD)
            aa_s = aa[:, TP:SCAN].rearrange("p (b j) -> p b j", j=NS + 1)
            with act.Fori(0, CC) as c:
                high(PAIR[1], c * 2)
                act.wait_ge(xr_done, c + 2)
                act.wait_ge(xcv_ready, c + 1)
                nc.scalar.activation(xrpad[:, RW - 1:RW - 1 + TH], halves[0][:, 0, :], ACT.Copy)
                nc.scalar.activation(xrpad[:, RW - 1 + TH:RW - 1 + TP], halves[0][:, 1, 0:TP - TH], ACT.Copy)
                nc.scalar.activation(xr_s[:, :, RW - 1:RPAD],
                                     halves[0][:, 1, TP - TH:TH].rearrange("p (b s) -> p b s", s=NS), ACT.Copy)
                nc.scalar.activation(xr_s[:, :, 0:RW - 1],
                                     par[:, c, R_SRC:R_SH].rearrange("p (b j) -> p b j", j=RW - 1),
                                     ACT.Copy).then_inc(xr_padded, 1)
                high(PAIR[0], c * 2 + 1)
                act.wait_ge(yr_done, c + 2)
                act.wait_ge(ha_ready, c + 1)
                nc.scalar.activation(yg.rearrange("p (a n) -> p a n", a=2), halves[1], ACT.Gelu_apprx_tanh).then_inc(yg_ready, 1)
                high(PAIR[1], c * 2 + 1)
                act.wait_ge(rgate_done, c + 1)
                nc.scalar.activation(rg, ps[:, 0, 0:T], ACT.Sigmoid, bias=par[:, c, R_BRG:R_BRG + 1]).then_inc(rg_ready, 1)
                act.wait_ge(igate_done, c + 2)
                nc.scalar.activation(ig, ps[:, 1, 0:T], ACT.Sigmoid, bias=par[:, c, R_BIG:R_BIG + 1]).then_inc(ig_ready, 1)
                high(PAIR[0], c * 2 + 2)
                act.wait_ge(rg_ready, c + 2)
                nc.scalar.activation(aa[:, 0:TP], rg[:, 0:TP], ACT.Exp, scale=cneg[:, bass.ds(c, 1)])
                nc.scalar.activation(aa_s[:, :, 1:NS + 1], rg[:, TP:T].rearrange("p (b s) -> p b s", s=NS),
                                     ACT.Exp, scale=cneg[:, bass.ds(c, 1)])
                nc.scalar.activation(th, rg, ACT.Tanh, scale=cpos[:, bass.ds(c, 1)]).then_inc(decay_ready, 1)
                act.wait_ge(beta2_ready, c + 1)
                nc.scalar.activation(t2, t1, ACT.Sqrt).then_inc(beta_ready, 1)
                act.wait_ge(cb_done, c + 2)
                act.wait_ge(glu_ready, c + 1)
                nc.scalar.activation(cg.rearrange("p (a n) -> p a n", a=2), halves[3], ACT.Sigmoid).then_inc(cg_ready, 1)

            def branch_gate(done, m, j, gate_ap, ready):
                act.wait_ge(done, m + 2)
                if j == 0:
                    act.wait_ge(merged_ready, m + 1)
                nc.scalar.activation(gate_ap.rearrange("p (a n) -> p a n", a=2), halves[j], ACT.Sigmoid).then_inc(ready, 1)

            def branch_turn(i, n, first=False):
                if not first:
                    high(PAIR[1], n)
                    branch_gate(ga_done, i * 2, 0, sga, sga_ready)
                    branch_gate(gb_done, i * 2, 1, sgb, sgb_ready)
                high(PAIR[1], n + 1)
                high(PAIR[0], n + 2)
                branch_gate(ga_done, i * 2 + 1, 0, sga, sga_ready)
                branch_gate(gb_done, i * 2 + 1, 1, sgb, sgb_ready)
                high(PAIR[0], n + 3)

            high(PAIR[1], USES[1])
            branch_gate(ga_done, 0, 0, sga, sga_ready)
            branch_gate(gb_done, 0, 1, sgb, sgb_ready)

            act.wait_ge(exT_done, 1)
            nc.scalar.activation(rows_out[0:E_N, :], ps[0:E_N, 3, :], ACT.Copy).then_inc(exT_read, 1)
            sqb = (th, t2)
            for c in range(CC):
                act.wait_ge(centered, c + 1)
                if c >= 2:
                    act.wait_ge(sq_used, c - 1)
                nc.scalar.activation(sqb[c % 2], dc[:, c, :], ACT.Square).then_inc(sq_ready, 1)
            act.wait_ge(sq_used, CC)
            nc.scalar.activation(rg.rearrange("p (a n) -> p a n", a=2), halves[1], ACT.Sqrt, bias=eps,
                                 scale=1.0 / CH).then_inc(sd_ready, 1)
            for c in range(CC):
                act.wait_ge(scaled, c + 1)
                nc.scalar.activation(dc[:, c, :], dc[:, c, :], ACT.Silu, scale=par[:, c, R_LNG:R_LNG + 1],
                                     bias=par[:, c, R_LNB:R_LNB + 1]).then_inc(silu_ready, 1)
            act.wait_ge(exT_read, 1)
            act.dma_start(cc_s[0, :, 0:CW - 1 - NS, :], state_cm_conv[0, :, NS:CW - 1, :]).then_inc(out_a, 16)
            for dst, r, n in [(rc_p.rearrange("l b j n -> (l b j) n"), E_RCP, 3),
                              (cc_p.rearrange("l b j n -> (l b j) n"), E_CCP, 30),
                              (h_p.rearrange("l b n -> (l b) n"), E_HP, 1),
                              (rc_s.rearrange("l b j n -> (l b j) n"), E_RCS, 24),
                              (h_s.rearrange("l b n -> (l b) n"), E_HS, 8)]:
                act.dma_start(dst, rows_out[r:r + n, :]).then_inc(out_a, 16)
            for b in range(NB):
                act.dma_start(cc_s[0, b, CW - 1 - NS:CW - 1, :],
                              rows_out[E_CCS + b * NS:E_CCS + (b + 1) * NS, :]).then_inc(out_a, 16)

            branch_turn(0, USES[1], first=True)
            with act.Fori(1, DC // 2) as i:
                branch_turn(i, i * 3 + USES[1])
            for m in range(DC):
                act.wait_ge(merged_ready, m + 2)
                nc.scalar.activation(xh[:, m, :], merged[:, m, :], ACT.Copy).then_inc(mhi_ready, 1)

            def widen(j):
                nc.scalar.activation(blockT[j][:, 0:TH], halves[j][:, 0, :], ACT.Copy)
                nc.scalar.activation(blockT[j][:, TH:TP], halves[j][:, 1, 0:TP - TH], ACT.Copy)
                return nc.scalar.activation(
                    blockT[j][:, TP:TX].rearrange("p (g t) -> p g t", g=4),
                    halves[j][:, 1, TP - TH:TH].unsqueeze(1).to_broadcast([P, 4, TS]), ACT.Copy)

            def out_block(i, j, ahead=True):
                if ahead:
                    high(PAIR[(j + 1) % 2], i * 2 + (USES[2] + (j + 1) // 2))
                act.wait_ge(out_done, i * 4 + (j + 3))
                act.wait_ge(outX_done[j % 2], i * 2 + j // 2 + 1)
                widen(j % 2).then_inc(outT_ready[j % 2], 1)

            with act.Fori(0, 3) as i:
                for j in range(4):
                    out_block(i, j)
            for j in range(4):
                out_block(3, j, ahead=j < 3)

            for j in range(2):
                act.wait_ge(x1_ready[j], DC // 2 + 1)
            act.dma_start(x1_d, reg_c).then_inc(x1_out, 16)
            for t in range(NT):
                sum_squares(t, xt, 1)
            root(2)
            for k in range(0, DC, 2):
                act.wait_ge(xT_done, DC + k + 1)
                nc.scalar.activation(xnT[:, k, :], ps[:, k % 4, 0:T], ACT.Copy).then_inc(xT_act, 1)

            sc32 = sc[:, 0:4 * HEADS].rearrange("p (t h) s k -> p t h s k", h=HEADS)

            def head(h):
                for j in range(2):
                    act.wait_ge(q_done, h * 2 + (j + 3))
                    act.wait_ge(s_done[j], h + 1)
                    widen(j).then_inc(qT_ready[j], 1)
                for j in range(2):
                    act.wait_ge(s_done[j], h + 2)
                    nc.scalar.activation(sc32[:, :, h, j, :],
                                         ps[:, 2 + j, 0:4 * NK].rearrange("p (t k) -> p t k", k=NK),
                                         ACT.Copy).then_inc(s_read[j], 1)

            def route_unit(u, scores_h=None):
                act.wait_ge(routed, u)
                if scores_h is not None:
                    for j in range(2):
                        act.wait_ge(s_read[j], scores_h + 2)
                part(act)
                nc.scalar.activation(scur, sc[:, u], ACT.Copy).then_inc(staged_scores, 1)
                act.wait_ge(top_ready, u + 1)
                nc.scalar.activation(ex16, sv, ACT.Exp, bias=nmax, accum_out=esum).then_inc(exp_ready, 1)

            def gelu_unit(u, parity):
                act.wait_ge(dot_done, u * TOPK + (TOPK + SLOTS))
                act.wait_ge(w_ready, u + 1)
                nc.scalar.activation(gel, dots[parity], ACT.Gelu_apprx_tanh).then_inc(gelu_ready, 1)

            def diagonals(v):
                act.wait_ge(w_ready, v + 2)
                for k in range(TOPK):
                    act.wait_ge(v_used, v * TOPK + (k + 1))
                    part(act)
                    nc.scalar.activation(diag[:, k, :], sel[:, v >> 5, :], ACT.Copy,
                                         scale=w_all[:, bass.ds(v * TOPK + k, 1)]).then_inc(diag_ready, 1)

            act.wait_ge(out_a, 16 * (6 + NB))
            head(0)
            route_unit(0, 0)
            with act.Fori(0, 3) as i:
                for n in range(2):
                    head(i * 2 + (n + 1))
                    route_unit(i * 2 + (n + 1), i * 2 + (n + 1))
                    gelu_unit(i * 2 + n, n)
            head(7)
            route_unit(7, 7)
            gelu_unit(6, 0)
            for j in range(2):
                act.wait_ge(s4_read[j], HEADS + 1)
            route_unit(8)
            gelu_unit(7, 1)
            with act.Fori(0, CATCH // 2) as i:
                for n in range(2):
                    u, v = i * 2 + (LEAD + n), i * 4 + 2 * n
                    diagonals(v)
                    route_unit(u + 1)
                    diagonals(v + 1)
                    gelu_unit(u, n)
            with act.Fori(0, (UNITS - LEAD - CATCH) // 2 - 1) as i:
                for n in range(2):
                    u = i * 2 + (LEAD + CATCH + n)
                    diagonals(u - SPARE)
                    route_unit(u + 1)
                    gelu_unit(u, n)
            diagonals(UNITS - 2 - SPARE)
            route_unit(UNITS - 1)
            gelu_unit(UNITS - 2, 0)
            diagonals(UNITS - 1 - SPARE)
            gelu_unit(UNITS - 1, 1)
            diagonals(UNITS - 2)
            act.wait_ge(acc_read, 4 * HEADS + 2)
            for t in range(NT - 1):
                sum_squares(t, xf, 2)
            root(3, slice(0, NT - 1))
            diagonals(UNITS - 1)
            act.wait_ge(acc_read, UNITS + 2)
            sum_squares(NT - 1, xf, 2)
            root(3, slice(NT - 1, NT))

        @block.vector
        def _(dve):
            for s in dve_counts:
                dve.sem_inc(s, 1)
            dve.sem_inc(dot_done, SLOTS)
            dve.sem_inc(acc_read, 2)
            step = Steps(dve, dve_step)
            mark, link = step.mark, step.link
            stt, tt, ts_ = nc.vector.scalar_tensor_tensor, nc.vector.tensor_tensor, nc.vector.tensor_scalar

            dve.wait_ge(rms_sqrt, 1)
            link(nc.vector.reciprocal(rstd, rstd))
            for t in range(NT):
                ts_(xt[:, t, :], xt[:, t, :], rstd[:, t:t + 1], None, ALU.mult).then_inc(xn_ready, 1)

            for k in range(DC):
                dve.wait_ge(xT_act, k + 1)
                stt(out=xl[:, k, :], in0=ps[:, k % 4, 0:T],
                    scalar=par[:, k % CC, R_GM + k // CC:R_GM + k // CC + 1], in1=xh_f[:, k, :],
                    op0=ALU.mult, op1=ALU.subtract).then_inc(xT_dve, 1)
            dve.wait_ge(staged_read, 1)
            lam_c = par[:, :, R_LAM]
            stt(out=sp_a, in0=lam_c, scalar=-1.0, in1=lam_c, op0=ALU.mult, op1=ALU.max).then_inc(lam_abs, 1)
            dve.wait_ge(exp_lam, 1)
            link(ts_(sp_c, sp_b, 2.0, None, ALU.add))
            link(nc.vector.reciprocal(sp_c, sp_c))
            link(tt(sp_b, sp_b, sp_c, ALU.mult))
            link(tt(sp_c, sp_b, sp_b, ALU.mult))
            link(ts_(sp_d, sp_c, 1.0 / 17, None, ALU.mult))
            for n in (15, 13, 11, 9, 7, 5, 3):
                link(stt(out=sp_d, in0=sp_d, scalar=1.0 / n, in1=sp_c, op0=ALU.add, op1=ALU.mult))
            link(stt(out=sp_d, in0=sp_d, scalar=1.0, in1=sp_b, op0=ALU.add, op1=ALU.mult))
            link(ts_(sp_a, lam_c, -1.0, 0.0, ALU.mult, ALU.max))
            link(stt(out=sp_d, in0=sp_d, scalar=2.0, in1=sp_a, op0=ALU.mult, op1=ALU.add))
            link(ts_(cpos, sp_d, LRU_C, None, ALU.mult))
            ts_(cneg, sp_d, -LRU_C, None, ALU.mult).then_inc(lru_ready, 1)

            xr_s = xrpad[:, RW - 1 + TP:RFLAT].rearrange("p (b j) -> p b j", j=RPAD)
            gl_s = glupad[:, CW - 1 + TP:CFLAT].rearrange("p (b j) -> p b j", j=CPAD)
            aa_s = aa[:, TP:SCAN].rearrange("p (b j) -> p b j", j=NS + 1)
            bb_s = bb[:, TP:SCAN].rearrange("p (b j) -> p b j", j=NS + 1)
            hh_s = hh[:, TP:SCAN].rearrange("p (b j) -> p b j", j=NS + 1)
            xc_s = xcv[:, TP + RW - 1:TP + RW - 1 + NB * RPAD].rearrange("p (b j) -> p b j", j=RPAD)[:, :, 0:NS]

            def bs(ap):
                return ap.rearrange("p (b s) -> p b s", s=NS)

            n4, n31 = RFLAT - RW + 1, CFLAT - CW + 1
            ac_s = acc31[:, TP + CW - 1:CFLAT].rearrange("p (b j) -> p b j", j=CPAD)[:, :, 0:NS]
            dve.wait_ge(const_ready, 1)
            dve.wait_ge(staged_read, 3)

            def short_conv(c):
                dve.wait_ge(xr_padded, c + 1)
                mark(nc.vector.tensor_copy(ex[:, c, E_RCP:E_RCP + 3], xrpad[:, TP:TP + RW - 1]))
                mark(nc.vector.tensor_copy(ex[:, c, E_RCS:E_RCS + 24].rearrange("p (b j) -> p b j", j=3),
                                           xr_s[:, :, NS:RPAD]))
                dve.wait_ge(igate_done, c + 1)
                link(ts_(xcv[:, 0:n4], xrpad[:, 0:n4], par[:, c, R_WR:R_WR + 1], par[:, c, R_BR:R_BR + 1],
                         ALU.mult, ALU.add))
                for k in range(1, RW):
                    ins = stt(out=xcv[:, 0:n4], in0=xrpad[:, k:k + n4], scalar=par[:, c, R_WR + k:R_WR + k + 1],
                              in1=xcv[:, 0:n4], op0=ALU.mult, op1=ALU.add)
                    if k < RW - 1:
                        link(ins)
                ins.then_inc(xcv_ready, 1)

            def recurrence_and_unit(c):
                dve.wait_ge(decay_ready, c + 1)
                mark(tt(t1[:, 0:TP], aa[:, 0:TP], aa[:, 0:TP], ALU.mult))
                link(tt(bs(t1[:, TP:T]), aa_s[:, :, 1:NS + 1], aa_s[:, :, 1:NS + 1], ALU.mult))
                stt(out=t1, in0=t1, scalar=1.0, in1=th, op0=ALU.add, op1=ALU.mult).then_inc(beta2_ready, 1)
                dve.wait_ge(xcv_ready, c + 2)
                dve.wait_ge(ig_ready, c + 2)
                mark(tt(bb[:, 0:TP], ig[:, 0:TP], xcv[:, 0:TP], ALU.mult))
                mark(tt(bb_s[:, :, 1:NS + 1], bs(ig[:, TP:T]), xc_s, ALU.mult))
                link(nc.vector.tensor_copy(bb_s[:, :, 0], par[:, c, R_SH:R_N]))
                dve.wait_ge(beta_ready, c + 1)
                mark(tt(bb[:, 0:TP], bb[:, 0:TP], t2[:, 0:TP], ALU.mult))
                link(tt(bb_s[:, :, 1:NS + 1], bb_s[:, :, 1:NS + 1], bs(t2[:, TP:T]), ALU.mult))
                link(nc.vector.tensor_tensor_scan(out=hh, data0=aa, data1=bb, initial=0.0, op0=ALU.mult, op1=ALU.add))
                mark(nc.vector.tensor_copy(ex[:, c, E_HP:E_HP + 1], hh[:, TP - 1:TP]))
                mark(nc.vector.tensor_copy(ex[:, c, E_HS:E_N], hh_s[:, :, NS]))
                dve.wait_ge(yg_ready, c + 1)
                mark(tt(ha[:, c, 0:TP], hh[:, 0:TP], yg[:, 0:TP], ALU.mult))
                tt(bs(ha[:, c, TP:T]), hh_s[:, :, 1:NS + 1], bs(yg[:, TP:T]), ALU.mult).then_inc(ha_ready, 1)
                dve.wait_ge(ca_done, c + 2)
                dve.wait_ge(cg_ready, c + 2)
                mark(nc.vector.tensor_copy(gl_s[:, :, 0:CW - 1], cmT[:, c, :].rearrange("p (b j) -> p b j", j=CW - 1)))
                mark(tt(glupad[:, CW - 1:CW - 1 + TH], halves[2][:, 0, :], cg[:, 0:TH], ALU.mult))
                mark(tt(glupad[:, CW - 1 + TH:CW - 1 + TP], halves[2][:, 1, 0:TP - TH], cg[:, TH:TP], ALU.mult))
                tt(gl_s[:, :, CW - 1:CPAD], bs(halves[2][:, 1, TP - TH:TH]), bs(cg[:, TP:T]), ALU.mult).then_inc(glu_ready, 1)
                dve.wait_ge(glu_ready, c + 2)
                mark(nc.vector.tensor_copy(ex[:, c, E_CCP:E_CCP + 30], glupad[:, TP:TP + CW - 1]))
                mark(nc.vector.tensor_copy(ex[:, c, E_CCS:E_CCS + TS].rearrange("p (b j) -> p b j", j=NS),
                                           gl_s[:, :, CW - 1:CPAD]))

            def long_conv(c):
                link(ts_(acc31[:, 0:n31], glupad[:, 0:n31], par[:, c, R_WC:R_WC + 1], par[:, c, R_BC:R_BC + 1],
                         ALU.mult, ALU.add))
                for k in range(1, CW - 1):
                    link(stt(out=acc31[:, 0:n31], in0=glupad[:, k:k + n31],
                             scalar=par[:, c, R_WC + k:R_WC + k + 1], in1=acc31[:, 0:n31],
                             op0=ALU.mult, op1=ALU.add))
                k = CW - 1
                w_k = par[:, c, R_WC + k:R_WC + k + 1]
                mark(stt(out=dc[:, c, 0:TP], in0=glupad[:, k:k + TP], scalar=w_k, in1=acc31[:, 0:TP],
                         op0=ALU.mult, op1=ALU.add))
                stt(out=bs(dc[:, c, TP:T]), in0=gl_s[:, :, k:CPAD], scalar=w_k, in1=ac_s,
                    op0=ALU.mult, op1=ALU.add).then_inc(dc_ready, 1)

            short_conv(0)
            recurrence_and_unit(0)
            with dve.Fori(0, CC - 1) as c:
                step.enter(c, PER_CHUNK)
                short_conv(c + 1)
                long_conv(c)
                recurrence_and_unit(c + 1)
                step.leave(CC - 1)
            long_conv(CC - 1)

            def two(ap):
                return ap.rearrange("p (a n) -> p a n", a=2)

            dve.wait_ge(mean_done, 1)
            ts_(two(t1), halves[0], -1.0 / CH, None, ALU.mult).then_inc(mean_read, 1)
            dve.wait_ge(mean_read, 1)
            for c in range(CC):
                tt(dc[:, c, :], dc[:, c, :], t1, ALU.add).then_inc(centered, 1)
            dve.wait_ge(sd_ready, 1)
            link(nc.vector.reciprocal(cg, rg))
            for c in range(CC):
                tt(dc[:, c, :], dc[:, c, :], cg, ALU.mult).then_inc(scaled, 1)

            with dve.Fori(0, DC) as m:
                step.enter(m, 1)
                dve.wait_ge(sga_ready, m + 2)
                dve.wait_ge(ba_done, m + 2)
                tt(two(sga), halves[2], two(sga), ALU.mult).then_inc(a_gated, 1)
                dve.wait_ge(sgb_ready, m + 2)
                dve.wait_ge(bb_done, m + 2)
                link(tt(two(sgb), halves[3], two(sgb), ALU.mult))
                tt(merged[:, m, :], sga, sgb, ALU.add).then_inc(merged_ready, 1)
                step.leave(DC)

            for m in range(DC):
                dve.wait_ge(mhi_ready, m + 1)
                tt(xl[:, m, :], merged[:, m, :], xh_f[:, m, :], ALU.subtract).then_inc(mlo_ready, 1)
            dve.wait_ge(x_again, 16 * (NT + 3))
            with dve.Fori(0, 4) as i:
                for j in range(4):
                    dve.wait_ge(outX_done[j % 2], i * 2 + j // 2 + 2)
                    col = xt[:, :, bass.ds(i * 4 * P + j * P, P)]
                    tt(col, col, ps[:, 2 + j % 2, 0:TX].rearrange("p (t n) -> p t n", n=P),
                       ALU.add).then_inc(x1_ready[j % 2], 1)

            dve.wait_ge(rms_sqrt, 2)
            link(nc.vector.reciprocal(rstd, rstd))
            dve.wait_ge(gffn_in, 16)
            for t in range(NT):
                stt(out=xn[:, t, :], in0=xt[:, t, :], scalar=rstd[:, t:t + 1], in1=gffn,
                    op0=ALU.mult, op1=ALU.mult).then_inc(xn_ready, 1)
            nc.vector.memset(sc[:, 4 * HEADS:UNITS], 0.0).then_inc(sc_zero, 1)
            for k in range(1, DC, 2):
                dve.wait_ge(xT_done, DC + k + 1)
                nc.vector.tensor_copy(xnT[:, k, :], ps[:, k % 4, 0:T]).then_inc(xT_dve, 1)

            dve.wait_ge(sc_zero, 1)

            def fifth_tile(h, n):
                for j in range(2):
                    dve.wait_ge(s_done[j], h + 2)
                    dve.wait_ge(s4_read[j], h + 1)
                    own = sc[:, 4 * HEADS + n, j, :]
                    stt(out=own, in0=ps[:, 2 + j, TP:TX], scalar=mask[:, bass.ds(h >> 1, 1)], in1=own,
                        op0=ALU.mult, op1=ALU.add).then_inc(s4_read[j], 1)

            def top16(vals, spare, out_v, out_i):
                part(dve)
                link(nc.vector.max(out_v[:, 0:8], vals), alone=True)
                mark(nc.vector.max_index(out_i[:, 0:8], out_v[:, 0:8], vals))
                link(nc.vector.match_replace(spare, out_v[:, 0:8], vals, LOW), alone=True)
                link(nc.vector.max(out_v[:, 8:16], spare), alone=True)
                link(nc.vector.max_index(out_i[:, 8:16], out_v[:, 8:16], spare))

            def route(u, parity):
                dve.wait_ge(staged_scores, u + 1)
                for s in range(2):
                    top16(scur[:, s, :], swork[:, s, :], top[:, s, :], topi[:, s, :])
                mark(nc.vector.tensor_copy(topf, topi))
                link(tt(cand.rearrange("p (a b) -> p a b", a=TOPK),
                        top[:, 0, :].unsqueeze(2).to_broadcast([P, TOPK, TOPK]),
                        top[:, 1, :].unsqueeze(1).to_broadcast([P, TOPK, TOPK]), ALU.add))
                top16(cand, cwork, sv, si)
                ts_(nmax, sv[:, 0:1], -1.0, None, ALU.mult).then_inc(top_ready, 1)
                mark(ts_(ab[:, 0, :], si, 4, None, ALU.logical_shift_right))
                link(ts_(ab[:, 1, :], si, 15, None, ALU.bitwise_and))
                link(nc.vector.tensor_copy(abf, ab.rearrange("p s k -> p (s k)")))
                eq3 = eq.rearrange("p (a c) -> p a c", c=TOPK)
                eq4 = eq.rearrange("p (s a c) -> p s a c", s=2, c=TOPK)
                link(tt(eq3, abf.unsqueeze(2).to_broadcast([P, 2 * TOPK, TOPK]),
                        iota_s.unsqueeze(1).to_broadcast([P, 2 * TOPK, TOPK]), ALU.is_equal))
                link(tt(eq4, eq4, topf.unsqueeze(2).to_broadcast([P, 2, TOPK, TOPK]), ALU.mult))
                link(nc.vector.tensor_reduce(ei.rearrange("p s k -> p (s k)"), eq3, AX.X, ALU.add))
                link(stt(out=idx_u[parity], in0=ei[:, 0, :], scalar=float(NK), in1=ei[:, 1, :],
                         op0=ALU.mult, op1=ALU.add))
                mark(nc.vector.tensor_copy(idx_all[:, bass.ds(u * TOPK, TOPK)], idx_u[parity]))
                dve.wait_ge(exp_ready, u + 1)
                link(nc.vector.reciprocal(ersum, esum))
                ts_(gate[parity], ex16, ersum, None, ALU.mult).then_inc(routed, 1)

            def dot(u, parity, k):
                s = k % SLOTS
                dve.wait_ge(u_landed[s], u * (16 * TOPK // SLOTS) + 16 * (k // SLOTS + 1))
                stt(out=ubuf[s], in0=ubuf[s], scalar=1.0, in1=xn[:, u >> 3, :], op0=ALU.mult,
                    op1=ALU.mult, accum_out=dots[parity][:, k:k + 1]).then_inc(dot_done, 1)

            def expert_weights(u, parity):
                dve.wait_ge(gelu_ready, u + 1)
                dve.wait_ge(routed, u + 1)
                tt(w_all[:, bass.ds(u * TOPK, TOPK)], gel, gate[parity], ALU.mult).then_inc(w_ready, 1)

            def add_unit(v, parity):
                dve.wait_ge(v_used, v * TOPK + 2 * TOPK)
                dve.wait_ge(acc_read, v + 2)
                tile_v = xf[:, v >> 3, :]
                tt(tile_v, tile_v, acc[parity], ALU.add).then_inc(acc_read, 1)

            def unit(u, parity, head_next=None, route_at=3, v_mid=None, v_end=None):
                for k in range(TOPK):
                    dot(u, parity, k)
                    if k == 3 and head_next is not None:
                        fifth_tile(head_next, 1 - parity)
                    if k == route_at:
                        route(u + 1, 1 - parity)
                    if k == 8 and v_mid is not None:
                        add_unit(v_mid, 0)
                expert_weights(u, parity)
                if v_end is not None:
                    add_unit(*v_end)

            fifth_tile(0, 0)
            route(0, 0)
            with dve.Fori(0, 3) as i:
                step.enter(i, 2 * PER_ROUTE)
                for n in range(2):
                    unit(i * 2 + n, n, head_next=i * 2 + (n + 1))
                step.leave(3)
            unit(6, 0, head_next=7)
            unit(7, 1)
            dve.wait_ge(x1_back, 16)
            with dve.Fori(0, CATCH // 2) as i:
                step.enter(i, 2 * PER_ROUTE)
                for n in range(2):
                    v = i * 4 + 2 * n
                    unit(i * 2 + (LEAD + n), n, route_at=1, v_mid=v, v_end=(v + 1, 1))
                step.leave(CATCH // 2)
            with dve.Fori(0, (UNITS - LEAD - CATCH) // 2 - 1) as i:
                step.enter(i, 2 * PER_ROUTE)
                for n in range(2):
                    u = i * 2 + (LEAD + CATCH + n)
                    unit(u, n, v_end=(u - SPARE, n))
                step.leave((UNITS - LEAD - CATCH) // 2 - 1)
            unit(UNITS - 2, 0, v_end=(UNITS - 2 - SPARE, 0))
            unit(UNITS - 1, 1, route_at=None, v_end=(UNITS - 1 - SPARE, 1))

            def normalised(tiles, n):
                dve.wait_ge(rms_sqrt, n)
                link(nc.vector.reciprocal(rstd[:, tiles], rstd[:, tiles]))
                for t in range(tiles.start, tiles.stop):
                    stt(out=xf[:, t, :], in0=xf[:, t, :], scalar=rstd[:, t:t + 1], in1=gfin,
                        op0=ALU.mult, op1=ALU.mult).then_inc(y_ready, 1)

            dve.wait_ge(gfin_in, 16)
            normalised(slice(0, NT - 1), 3)
            for v in range(UNITS - SPARE, UNITS):
                add_unit(v, v % 2)
            normalised(slice(NT - 1, NT), 4)

        @block.tensor
        def _(pe):
            for s in pe_counts:
                pe.sem_inc(s, 1)
            pe.sem_inc(v_used, TOPK)
            pe.sem_inc(out_done, 2)
            pe.sem_inc(q_done, 2)
            mm, tr = nc.tensor.matmul, nc.tensor.transpose
            pe.wait_ge(const_ready, 1)
            pe.wait_ge(rows_in, 16 * 12)
            for c in range(CC):
                o = 512 * (c // 4) + R_N * (c % 4)
                last = tr(ps[:, 2, o:o + R_N], rows[0:R_N, c * P:(c + 1) * P], ident[0:R_N, 0:R_N])
            last.then_inc(stagedT, 1)

            def tokens_to_channels(done, x):
                pe.wait_ge(xn_ready, (done + 1) * NT)
                for k in range(DC):
                    if k >= 4:
                        if not done:
                            pe.wait_ge(xT_dve, k - 3)
                        else:
                            pe.wait_ge(xT_dve if k % 2 else xT_act, DC + (k - 4) // 2 + 1)
                    if k == 2 and not done:
                        pe.wait_ge(staged_read, 1)
                    for t in range(NT - 1):
                        tr(ps[:, k % 4, t * P:(t + 1) * P], x[:, t, k * P:(k + 1) * P], ident)
                    tr(ps[:, k % 4, TP:T], x[0:TS, NT - 1, k * P:(k + 1) * P],
                       ident[0:TS, 0:TS]).then_inc(xT_done, 1)
                pe.wait_ge(xT_act, DC + done * DC // 2)
                pe.wait_ge(xT_dve, DC + done * DC // 2)

            tokens_to_channels(0, xt)
            pe.wait_ge(cm_in, 32)
            for n in range(2):
                for c in range(4):
                    for a in range(2):
                        o = 512 * (c // 2) + 240 * (c % 2) + 120 * a
                        last = tr(ps[:, n, o:o + 120], cmrows[0:120, a, (4 * n + c) * P:(4 * n + c + 1) * P],
                                  ident[0:120, 0:120])
                last.then_inc(stagedT, 1)
            pe.wait_ge(keys_in, 32)
            for s in range(2):
                for h in range(HEADS):
                    last = tr(ps[:, 2 + s, h * P:(h + 1) * P], krows[:, s, h, :], ident)
                last.then_inc(stagedT, 1)
            pe.wait_ge(staged_read, 2)

            def product3(j, pair, n, ready=None):
                for half, s in enumerate(PAIR[pair]):
                    pe.wait_ge(lo_ready[s], n + 1)
                    for q in range(KP):
                        k = half * KP + q
                        if ready is not None:
                            pe.wait_ge(ready, k + 1)
                        hi, lo = whi[s][:, q * P:(q + 1) * P], wlo[s][:, q * P:(q + 1) * P]
                        for a in range(2):
                            h = slice(a * TH, (a + 1) * TH)
                            mm(halves[j][:, a, :], hi, xh[:, k, h], start=(k == 0), stop=False)
                            mm(halves[j][:, a, :], hi, xl[:, k, h], start=False, stop=False)
                            last = mm(halves[j][:, a, :], lo, xh[:, k, h], start=False, stop=(k == DC - 1))
                    if half == 0:
                        last.then_inc(half_used[pair], 1)
                return last

            def product(j, slots, n, rhs, used=None, ready=None):
                chunks = KP * len(slots)
                for half, s in enumerate(slots):
                    pe.wait_ge(w_landed[s], n * 16 + 16)
                    for q in range(KP):
                        k = half * KP + q
                        if ready is not None:
                            pe.wait_ge(ready, k + 1)
                        for a in range(2):
                            last = mm(halves[j][:, a, :], wraw[s][:, q * P:(q + 1) * P],
                                      rhs[:, k, a * TH:(a + 1) * TH], start=(k == 0), stop=(k == chunks - 1))
                    if half < len(slots) - 1:
                        last.then_inc(used, 1)
                return last

            xc_s = xcv[:, TP + RW - 1:TP + RW - 1 + NB * RPAD].rearrange("p (b j) -> p b j", j=RPAD)[:, :, 0:NS]
            with pe.Fori(0, CC) as c:
                pe.wait_ge(rg_ready, c + 1)
                product3(0, 0, c * 2).then_inc(xr_done, 1)
                pe.wait_ge(staged_read, 5)
                pe.wait_ge(ig_ready, c + 1)
                product3(1, 1, c * 2).then_inc(yr_done, 1)
                pe.wait_ge(glu_ready, c + 1)
                product3(2, 0, c * 2 + 1).then_inc(ca_done, 1)
                pe.wait_ge(gw_landed, c * 32 + 32)
                pe.wait_ge(xcv_ready, c + 2)
                for s, (read, done) in enumerate(((xr_padded, rgate_done), (yg_ready, igate_done))):
                    pe.wait_ge(read, c + 1)
                    mm(ps[:, s, 0:TP], gw[:, s, :], xcv[:, 0:TP], start=True, stop=True)
                    mm(ps[:, s, TP:T].rearrange("p (b s) -> p b s", s=NS), gw[:, s, :], xc_s,
                       start=True, stop=True).then_inc(done, 1)
                pe.wait_ge(cg_ready, c + 1)
                product3(3, 1, c * 2 + 1).then_inc(cb_done, 1)

            def branch_block(m, use, q, pair):
                pe.wait_ge(sga_ready, m + 1)
                product3(0, pair, q).then_inc(ga_done, 1)
                pe.wait_ge(sgb_ready, m + 1)
                product3(1, 1 - pair, q).then_inc(gb_done, 1)
                pe.wait_ge(a_gated, m + 1)
                product(2, PAIR[pair][0:1], use, ha).then_inc(ba_done, 1)
                pe.wait_ge(merged_ready, m + 1)
                product(3, PAIR[pair][1:2], use, dc).then_inc(bb_done, 1)

            pe.wait_ge(rg_ready, CC + 1)
            product3(0, 0, SPLITS[1]).then_inc(ga_done, 1)
            pe.wait_ge(ig_ready, CC + 1)
            product3(1, 1, SPLITS[1]).then_inc(gb_done, 1)
            pe.wait_ge(ha_ready, CC + 1)
            pe.wait_ge(glu_ready, CC + 1)
            product(2, PAIR[0][0:1], USES[1] + 1, ha).then_inc(ba_done, 1)
            pe.wait_ge(dc_ready, CC)
            pe.wait_ge(sga_ready, 2)
            for c in range(CC):
                for a in range(2):
                    last = mm(halves[0][:, a, :], ones, dc[:, c, a * TH:(a + 1) * TH],
                              start=(c == 0), stop=(c == CC - 1))
            last.then_inc(mean_done, 1)
            pe.wait_ge(cg_ready, CC + 1)
            for c in range(CC):
                last = tr(ps[0:E_N, 3, c * P:(c + 1) * P], ex[:, c, :], ident)
            last.then_inc(exT_done, 1)
            pe.wait_ge(sgb_ready, 2)
            sqb = (th, t2)
            for c in range(CC):
                pe.wait_ge(sq_ready, c + 1)
                for a in range(2):
                    last = mm(halves[1][:, a, :], ones, sqb[c % 2][:, a * TH:(a + 1) * TH],
                              start=(c == 0), stop=(c == CC - 1))
                last.then_inc(sq_used, 1)
            pe.wait_ge(exT_read, 1)
            product(3, PAIR[0][1:2], USES[1] + 1, dc, ready=silu_ready).then_inc(bb_done, 1)
            pe.wait_ge(mean_read, 1)
            pe.wait_ge(sd_ready, 1)
            branch_block(1, USES[1] + 2, SPLITS[1] + 1, 1)
            with pe.Fori(1, DC // 2) as i:
                n, q = i * 3 + USES[1], i * 2 + SPLITS[1]
                branch_block(i * 2, n + 1, q, 0)
                branch_block(i * 2 + 1, n + 2, q + 1, 1)

            def back_to_tokens(i, j):
                pe.wait_ge(outT_ready[j % 2], i * 2 + j // 2 + 2)
                pe.wait_ge(x1_ready[j % 2], i * 2 + j // 2 + 1)
                for t in range(NT):
                    last = tr(ps[:, 2 + j % 2, t * P:(t + 1) * P], blockT[j % 2][:, t * P:(t + 1) * P], ident)
                last.then_inc(outX_done[j % 2], 1)

            def score(h, j):
                pe.wait_ge(qT_ready[j], h + 2)
                pe.wait_ge(s_read[j], h + 1)
                pe.wait_ge(s4_read[j], h + 1)
                for t in range(NT):
                    last = mm(ps[:, 2 + j, t * P:(t + 1) * P], blockT[j][:, t * P:(t + 1) * P],
                              keysT[:, j, h, :], start=True, stop=True)
                last.then_inc(s_done[j], 1)

            pe.wait_ge(merged_ready, DC + 1)
            with pe.Fori(0, 4) as i:
                for j in range(4):
                    pe.wait_ge(outT_ready[j % 2], i * 2 + j // 2 + 1)
                    product3(j % 2, j % 2, i * 2 + (SPLITS[2] + j // 2),
                             mlo_ready if j == 0 else None).then_inc(out_done, 1)
                    if j:
                        back_to_tokens(i, j - 1)
                back_to_tokens(i, 3)
            tokens_to_channels(1, xn)
            with pe.Fori(0, HEADS // 2) as i:
                for n in range(2):
                    h = i * 2 + n
                    for j in range(2):
                        pe.wait_ge(qT_ready[j], h + 1)
                        product(j, PAIR[j], i * 2 + (USES[3] + n), xnT, half_used[j]).then_inc(q_done, 1)
                    score(h, 0)
                    score(h, 1)

            for j in range(2):
                pe.wait_ge(s4_read[j], HEADS + 1)
                pe.wait_ge(s_read[j], HEADS + 1)
                pe.wait_ge(qT_ready[j], HEADS + 1)
            with pe.Fori(0, UNITS // 2) as i:
                for n in range(2):
                    v = i * 2 + n
                    pe.wait_ge(acc_read, v + 1)
                    for k in range(TOPK):
                        s = k % SLOTS
                        pe.wait_ge(diag_ready, v * TOPK + (k + 1))
                        pe.wait_ge(v_landed[s], v * (16 * TOPK // SLOTS) + 16 * (k // SLOTS + 1))
                        for b in range(4):
                            last = mm(acc[n][:, b * 512:(b + 1) * 512], diag[:, k, :],
                                      vbuf[s][:, b * 512:(b + 1) * 512], start=(k == 0), stop=(k == TOPK - 1))
                        last.then_inc(v_used, 1)


_INS = ['x_prompt', 'x_sample', 'state_rnn_conv', 'state_rnn_h', 'state_cm_conv', 'g_mix', 'w_in',
        'w_rconv', 'b_rconv', 'w_r', 'b_r', 'w_i', 'b_i', 'lam', 'w_a', 'w_cconv', 'b_cconv', 'ln_g',
        'ln_b', 'w_b', 'w_out', 'g_ffn', 'w_q', 'keys1', 'keys2', 'u_tab', 'v_tab', 'g_final']
_OUTS = [(1, TP, D), (NB, NS, D), (1, 1, RW - 1, CH), (1, 1, CH), (1, 1, CW - 1, CH),
         (1, NB, RW - 1, CH), (1, NB, CH), (1, NB, CW - 1, CH)]


def kernel(**inputs):
    import numpy as _np
    import concourse.bacc as _bacc
    from concourse.bass_utils import run_bass_kernel_spmd as _run

    nc = _bacc.Bacc("TRN2", target_bir_lowering=False, num_devices=1)
    arrays, args = {}, []
    for name in _INS:
        a = _np.ascontiguousarray(inputs[name])
        arrays[f"in_{name}_dram"] = a
        args.append(nc.dram_tensor(f"in_{name}_dram", a.shape, mybir.dt.from_np(a.dtype), kind="ExternalInput").ap())
    for i, shape in enumerate(_OUTS):
        args.append(nc.dram_tensor(f"out_{i}_dram", shape, F32, kind="ExternalOutput").ap())
    hybrid_step(nc, *args)
    r = _run(nc, [arrays], core_ids=[0])
    return tuple(r.results[0][f"out_{i}_dram"] for i in range(len(_OUTS)))
```
